# Optimizing a Trainium2 kernel written in Bass

```python
import math
import jax, jax.numpy as jnp
from jax import lax
import numpy as np

D_MODEL = 1024
BATCH = 1
SEQ = 512
DEPTH = 1

CONV_CH = 512
CONV_K = 3
N_HEADS = 8
HEAD_DIM = 64
N_KV = 2
HPG = N_HEADS // N_KV
ATTN_W = N_HEADS * HEAD_DIM
KV_W = N_KV * HEAD_DIM
MIX_W = CONV_CH + ATTN_W
CMP_BLOCK = 32
CMP_STRIDE = 16
CMP_HIDDEN = 256
SEL_BLOCK = 64
SEL_TOP = 16
WINDOW = 512
Q_BLOCK = 64
N_GATES = 3 * N_HEADS
PEER_HEADS = 8
PEER_NKEYS = 128
PEER_EXPERTS = PEER_NKEYS * PEER_NKEYS
PEER_DKEY = 256
PEER_TOPK = 16
PEER_CHUNK = 128

EPS = 1e-6
NEG_INF = -1e30
FORCE = 1e4

COL_SIZES = [CONV_CH, CONV_CH, CONV_CH, ATTN_W, KV_W, KV_W, KV_W, KV_W, KV_W, KV_W, N_GATES]
IN_COLS = sum(COL_SIZES)
SPLIT_POINTS = list(np.cumsum(COL_SIZES)[:-1])

kernel_name = "hybrid_conv_nsa_peer_layer"

def rms_norm(x, g):
    x32 = x.astype(jnp.float32)
    y = x32 * lax.rsqrt(jnp.mean(x32 * x32, axis=-1, keepdims=True) + EPS)
    return (y * g.astype(jnp.float32)).astype(x.dtype)

def masked_softmax(s, valid):
    s = jnp.where(valid, s.astype(jnp.float32), NEG_INF)
    return jax.nn.softmax(s, axis=-1)

def short_conv(z, w):
    c = z.shape[-1]
    return lax.conv_general_dilated(
        z, w[:, None, :].astype(z.dtype), window_strides=(1,),
        padding=[(CONV_K - 1, 0)], dimension_numbers=("NWC", "WIO", "NWC"),
        feature_group_count=c)

def compress_blocks(k, pos, w1, w2):
    b, s = k.shape[0], k.shape[1]
    n_cmp = (s - CMP_BLOCK) // CMP_STRIDE + 1
    idx = (jnp.arange(n_cmp) * CMP_STRIDE)[:, None] + jnp.arange(CMP_BLOCK)[None, :]
    blocks = k[:, idx] + pos[None, None, :, None, :]
    flat = blocks.transpose(0, 1, 3, 2, 4).reshape(b, n_cmp, N_KV, CMP_BLOCK * HEAD_DIM)
    return jax.nn.gelu(flat @ w1) @ w2

def nsa(q, kc, vc, ks, vs, kw, vw, gates):
    b, s = q.shape[0], q.shape[1]
    dt = q.dtype
    n_cmp = kc.shape[1]
    n_sel = s // SEL_BLOCK
    n_top = min(SEL_TOP, n_sel)
    scale = HEAD_DIM ** -0.5
    cmp_start = jnp.arange(n_cmp) * CMP_STRIDE
    cmp_end = cmp_start + CMP_BLOCK - 1
    sel_start = jnp.arange(n_sel) * SEL_BLOCK
    overlap = ((cmp_start[:, None] < sel_start[None, :] + SEL_BLOCK)
               & (cmp_start[:, None] + CMP_BLOCK > sel_start[None, :])).astype(jnp.float32)
    ks_blk = ks.reshape(b, n_sel, SEL_BLOCK, N_KV, HEAD_DIM).transpose(0, 3, 1, 2, 4)
    vs_blk = vs.reshape(b, n_sel, SEL_BLOCK, N_KV, HEAD_DIM).transpose(0, 3, 1, 2, 4)
    kw_pad = jnp.pad(kw, ((0, 0), (WINDOW, 0), (0, 0), (0, 0)))
    vw_pad = jnp.pad(vw, ((0, 0), (WINDOW, 0), (0, 0), (0, 0)))
    gather_blocks = jax.vmap(jax.vmap(lambda kb, ix: kb[ix]))
    j = jnp.arange(n_sel)

    def block(i):
        t0 = i * Q_BLOCK
        tq = t0 + jnp.arange(Q_BLOCK)
        qb = lax.dynamic_slice_in_dim(q, t0, Q_BLOCK, axis=1).reshape(b, Q_BLOCK, N_KV, HPG, HEAD_DIM)
        s_c = jnp.einsum('bqghd,bngd->bghqn', qb, kc).astype(jnp.float32) * scale
        valid_c = cmp_end[None, :] <= tq[:, None]
        has_c = jnp.any(valid_c, axis=-1).astype(jnp.float32)[:, None]
        p_c = masked_softmax(s_c, valid_c) * has_c
        o_c = jnp.einsum('bghqn,bngd->bqghd', p_c.astype(dt), vc)
        imp = jnp.einsum('bghqn,nj->bgqj', p_c, overlap)
        qblk = tq // SEL_BLOCK
        forced = (j[None, :] == 0) | (j[None, :] == qblk[:, None]) | (j[None, :] == qblk[:, None] - 1)
        imp = jnp.where(j[None, :] > qblk[:, None], -FORCE, imp + jnp.where(forced, FORCE, 0.0))
        _, sel = lax.top_k(imp, n_top)
        k_sel = gather_blocks(ks_blk, sel)
        v_sel = gather_blocks(vs_blk, sel).reshape(b, N_KV, Q_BLOCK, n_top * SEL_BLOCK, HEAD_DIM)
        kpos = sel[..., None] * SEL_BLOCK + jnp.arange(SEL_BLOCK)
        valid_s = (kpos <= tq[None, None, :, None, None]).reshape(b, N_KV, Q_BLOCK, n_top * SEL_BLOCK)
        s_s = jnp.einsum('bqghd,bgqnkd->bghqnk', qb, k_sel).reshape(
            b, N_KV, HPG, Q_BLOCK, n_top * SEL_BLOCK).astype(jnp.float32) * scale
        p_s = masked_softmax(s_s, valid_s[:, :, None])
        o_s = jnp.einsum('bghqm,bgqmd->bqghd', p_s.astype(dt), v_sel)
        kwb = lax.dynamic_slice_in_dim(kw_pad, t0, WINDOW + Q_BLOCK, axis=1)
        vwb = lax.dynamic_slice_in_dim(vw_pad, t0, WINDOW + Q_BLOCK, axis=1)
        tk = t0 - WINDOW + jnp.arange(WINDOW + Q_BLOCK)
        valid_w = (tk[None, :] <= tq[:, None]) & (tk[None, :] > tq[:, None] - WINDOW) & (tk[None, :] >= 0)
        s_w = jnp.einsum('bqghd,bkgd->bghqk', qb, kwb).astype(jnp.float32) * scale
        p_w = masked_softmax(s_w, valid_w)
        o_w = jnp.einsum('bghqk,bkgd->bqghd', p_w.astype(dt), vwb)
        g = lax.dynamic_slice_in_dim(gates, t0, Q_BLOCK, axis=1).reshape(b, Q_BLOCK, N_KV, HPG, 3).astype(dt)
        o = g[..., 0:1] * o_c + g[..., 1:2] * o_s + g[..., 2:3] * o_w
        return o.reshape(b, Q_BLOCK, ATTN_W)

    out = lax.map(block, jnp.arange(s // Q_BLOCK))
    return out.transpose(1, 0, 2, 3).reshape(b, s, ATTN_W)

def peer(xn, wq, subkeys, u, v):
    b, s, d = xn.shape
    t = b * s
    xt = xn.reshape(t, d)
    q = (xt @ wq).reshape(t, PEER_HEADS, 2, PEER_DKEY // 2)
    sc = jnp.einsum('thcd,hcnd->thcn', q, subkeys).astype(jnp.float32)
    sv, si = lax.top_k(sc, PEER_TOPK)
    cand = (sv[:, :, 0, :, None] + sv[:, :, 1, None, :]).reshape(t, PEER_HEADS, PEER_TOPK * PEER_TOPK)
    best, bi = lax.top_k(cand, PEER_TOPK)
    i1 = jnp.take_along_axis(si[:, :, 0], bi // PEER_TOPK, axis=-1)
    i2 = jnp.take_along_axis(si[:, :, 1], bi % PEER_TOPK, axis=-1)
    eidx = (i1 * PEER_NKEYS + i2).reshape(t, PEER_HEADS * PEER_TOPK)
    gate = jax.nn.softmax(best, axis=-1).reshape(t, PEER_HEADS * PEER_TOPK).astype(xn.dtype)
    n_c = t // PEER_CHUNK

    def chunk(args):
        xc, ec, gc = args
        h = jnp.einsum('td,tkd->tk', xc, u[ec])
        a = gc * jax.nn.gelu(h)
        return jnp.einsum('tk,tkd->td', a, v[ec])

    out = lax.map(chunk, (xt.reshape(n_c, PEER_CHUNK, d),
                          eidx.reshape(n_c, PEER_CHUNK, PEER_HEADS * PEER_TOPK),
                          gate.reshape(n_c, PEER_CHUNK, PEER_HEADS * PEER_TOPK)))
    return out.reshape(b, s, d)

def setup_inputs(seed: int = 0) -> dict:
    key = jax.random.key(seed)
    ks = jax.random.split(key, 20)
    f32 = jnp.float32
    nrm = lambda k, shape, sc: jax.random.normal(k, shape, f32) * sc
    L = DEPTH
    return {
        "x": nrm(ks[0], (BATCH, SEQ, D_MODEL), 1.0),
        "ln1": 1.0 + nrm(ks[1], (L, D_MODEL), 0.02),
        "w_in": nrm(ks[2], (L, D_MODEL, IN_COLS), D_MODEL ** -0.5),
        "conv_w": nrm(ks[3], (L, CONV_K, CONV_CH), CONV_K ** -0.5),
        "cmp_pos_k": nrm(ks[4], (L, CMP_BLOCK, HEAD_DIM), 0.1),
        "cmp_pos_v": nrm(ks[5], (L, CMP_BLOCK, HEAD_DIM), 0.1),
        "cmp_k_w1": nrm(ks[6], (L, CMP_BLOCK * HEAD_DIM, CMP_HIDDEN), (CMP_BLOCK * HEAD_DIM) ** -0.5),
        "cmp_k_w2": nrm(ks[7], (L, CMP_HIDDEN, HEAD_DIM), CMP_HIDDEN ** -0.5),
        "cmp_v_w1": nrm(ks[8], (L, CMP_BLOCK * HEAD_DIM, CMP_HIDDEN), (CMP_BLOCK * HEAD_DIM) ** -0.5),
        "cmp_v_w2": nrm(ks[9], (L, CMP_HIDDEN, HEAD_DIM), CMP_HIDDEN ** -0.5),
        "gn_conv": 1.0 + nrm(ks[10], (L, CONV_CH), 0.02),
        "gn_attn": 1.0 + nrm(ks[11], (L, ATTN_W), 0.02),
        "w_out": nrm(ks[12], (L, MIX_W, D_MODEL), MIX_W ** -0.5),
        "ln2": 1.0 + nrm(ks[13], (L, D_MODEL), 0.02),
        "peer_wq": nrm(ks[14], (L, D_MODEL, PEER_HEADS * PEER_DKEY), D_MODEL ** -0.5),
        "peer_subkeys": nrm(ks[15], (L, PEER_HEADS, 2, PEER_NKEYS, PEER_DKEY // 2), (PEER_DKEY // 2) ** -0.5),
        "peer_u": nrm(ks[16], (L, PEER_EXPERTS, D_MODEL), D_MODEL ** -0.5),
        "peer_v": nrm(ks[17], (L, PEER_EXPERTS, D_MODEL), 0.5),
        "ln_f": 1.0 + nrm(ks[18], (D_MODEL,), 0.02),
    }

def reference(x, ln1, w_in, conv_w, cmp_pos_k, cmp_pos_v, cmp_k_w1, cmp_k_w2, cmp_v_w1, cmp_v_w2,
              gn_conv, gn_attn, w_out, ln2, peer_wq, peer_subkeys, peer_u, peer_v, ln_f):
    b, s, _ = x.shape
    h = x
    for l in range(DEPTH):
        xn = rms_norm(h, ln1[l])
        proj = xn @ w_in[l]
        c_h, c_b, c_c, q, kc, vc, ksl, vsl, kwn, vwn, g = jnp.split(proj, SPLIT_POINTS, axis=-1)
        conv_out = c_b * short_conv(c_c * c_h, conv_w[l])
        r = lambda t: t.reshape(b, s, N_KV, HEAD_DIM)
        kc_c = compress_blocks(r(kc), cmp_pos_k[l], cmp_k_w1[l], cmp_k_w2[l])
        vc_c = compress_blocks(r(vc), cmp_pos_v[l], cmp_v_w1[l], cmp_v_w2[l])
        gates = jax.nn.sigmoid(g.astype(jnp.float32)).reshape(b, s, N_HEADS, 3)
        attn_out = nsa(q.reshape(b, s, N_HEADS, HEAD_DIM), kc_c, vc_c, r(ksl), r(vsl), r(kwn), r(vwn), gates)
        mix = jnp.concatenate([rms_norm(conv_out, gn_conv[l]), rms_norm(attn_out, gn_attn[l])], axis=-1)
        h = h + mix @ w_out[l]
        h = h + peer(rms_norm(h, ln2[l]), peer_wq[l], peer_subkeys[l], peer_u[l], peer_v[l])
    return rms_norm(h, ln_f)


_drawn_inputs = setup_inputs


def setup_inputs(seed=0):
    import zlib

    import numpy as np

    out = dict(_drawn_inputs(seed))
    spreads = {}
    factors = {'cmp_pos_k': 2.694, 'ln_f': 2.903}
    for name, (base, spread) in spreads.items():
        noise = np.random.default_rng([zlib.crc32(name.encode()), seed]).standard_normal(out[name].shape)
        drawn = base * np.exp(spread * noise) if base else spread * noise
        out[name] = __import__('jax').numpy.asarray(drawn.astype(out[name].dtype))
    for name, factor in factors.items():
        out[name] = (out[name] * factor).astype(out[name].dtype)
    return out
```

```python
from contextlib import ExitStack

import numpy as np

import concourse.bass as bass
from concourse import mybir

F32 = mybir.dt.float32
U32 = mybir.dt.uint32
ALU = mybir.AluOpType
ACT = mybir.ActivationFunctionType
AX_X = mybir.AxisListType.X

P = 128
SEQ, D = 512, 1024
TILES = SEQ // P
DC = D // P
HEADS, GROUPS, HD = 8, 2, 64
HPG = HEADS // GROUPS
NB = 32
NCMP = (SEQ - 32) // 16 + 1
LPAIRS = 16
CC = 4
PH = 8
HC = 2 * PH
TOPK = 16
KTOT = PH * TOPK
EPS = 1e-6
NEG = -1e30
GELU_C = float(np.sqrt(2.0 / np.pi))
RING = 8
GRP = 4
ITERS = KTOT // RING
SLOTS = 4

STREAM1 = (["kc", "vc", "ks", "kw", "q0", "q1", "q2", "q3", "vs", "vw"]
           + [f"w1k{i}" for i in range(4)] + [f"w1v{i}" for i in range(4)]
           + [f"{s}{c}" for c in range(CC) for s in "hcb"])
N1 = len(STREAM1)

BRANCH_HEADS = [(b, h) for b in range(2) for h in (0, 4, 1, 5, 2, 6, 3, 7)]
NBH = len(BRANCH_HEADS)

PIECES = (["cmp_scores", "cmp_out"] + [f"att{i}" for i in range(NBH // 2 + 1)]
          + ["mix", "norm2"] + [f"query{i}" for i in range(4)] + ["topk3"])


def wide_order():
    names = ["kc", "vc", "ks", "kw", "q0", "q1", "q2", "q3", "vs", "vw", "gt", "hidk", "hidv", "h0", "c0", "b0",
             "kcc", "vcc"] + [f"{s}{c}" for c in range(1, CC) for s in "hcb"]
    for t in range(TILES):
        names += [("sc", t, g) for g in range(GROUPS)] + [("oc", t)]
        names += [("s", t, n) for n in range(NBH)]
        names += [("yc", t, 0), ("ya", t, 0), ("yc", t, 1), ("ya", t, 1), ("g2", t, 0), ("g2", t, 1)]
        for i in range(4):
            names += [("pq", t, i), ("ps", t, i)]
    return {name: n for n, name in enumerate(names)}


def turn_order():
    names = [("x", t, i) for t in range(TILES) for i in range(2)]
    for t in range(TILES):
        names += [("pc", t)] + [("p", t, n) for n in range(NBH)] + [("at", t), ("x2", t, 0), ("x2", t, 1)]
    return {name: n for n, name in enumerate(names)}


def layer(nc, A, out):
    WIDE, TURN = wide_order(), turn_order()
    with ExitStack() as ctx:
        def sb(name, shape, dt=F32):
            return ctx.enter_context(nc.sbuf_tensor(name, shape, dt))

        def sem(name):
            return ctx.enter_context(nc.semaphore(name))

        wide = ctx.enter_context(nc.psum_tensor("wide", [P, 2, 512], F32))
        turn = ctx.enter_context(nc.psum_tensor("turn", [P, 2, 512], F32))
        att_ps = ctx.enter_context(nc.psum_tensor("att_ps", [P, 2, 512], F32))
        acc = ctx.enter_context(nc.psum_tensor("acc", [P, 2, 512], F32))

        ring = sb("ring", [P, RING, 2 * D])
        stream = sb("stream", [P, SLOTS, D])
        w_out = sb("w_out_sb", [P, DC, D])
        subk = sb("subk", [P, HC, P])
        qT = sb("qT", [P, HPG, SEQ])
        kT = sb("kT", [P, 2, SEQ])
        vtok = sb("vtok", [P, TILES, 2, P])
        convT = sb("convT", [P, CC, SEQ])
        ln2row = sb("ln2row", [1, D])
        lnf = sb("lnf", [P, D])
        xh = sb("xh", [P, 2, D])
        xn2 = sb("xn2", [P, 2, D])
        ident = sb("ident", [P, P])
        causal = sb("causal", [P, P])
        cmask = sb("cmask", [P, TILES, NB])
        has_c = sb("has_c", [P, 1])
        iota16 = sb("iota16", [P, TOPK])
        iota16i = sb("iota16i", [P, TOPK], mybir.dt.int32)
        ones_row = sb("ones_row", [1, P])
        mean_col = sb("mean_col", [P, 1])
        ln1 = sb("ln1_sb", [P, DC])
        convw = sb("convw", [P, CC, 3])
        gnc = sb("gnc", [P, CC])
        gna = sb("gna", [P, CC])
        pos = sb("pos", [P, 2, LPAIRS])
        w2k = sb("w2k", [P, 2, P])
        w2v = sb("w2v", [P, 2, HD])
        wg = sb("wg", [P, DC, 24])
        sig = sb("sig", [P, TILES, 3, HEADS])
        kcc = sb("kcc", [P, NB])
        vbd = sb("vbd", [P, GROUPS, HPG, HD])
        stat = sb("stat", [P, 8])
        newton = sb("newton", [P, 3, TILES])
        rstd_c = sb("rstd_c", [P, TILES])
        hx = sb("hx", [P, 2, 2, 62])
        ht = sb("ht", [P, 2, 2, 62])
        hbias = sb("hbias", [P, 2, 2])
        hidk = sb("hidk", [P, 2, GROUPS, NB])
        hidv = sb("hidv", [P, 2, GROUPS, HPG, NB])
        probs = sb("probs", [P, 2, 512])
        probsT = sb("probsT", [P, 2, 512])
        attn = sb("attn", [P, 512])
        atmp = sb("atmp", [P, 512])
        attT = sb("attT", [P, 512])
        xT2 = probs[:, :, :].rearrange("p a b -> p (a b)")
        pq = probsT
        pcs = sb("pcs", [P, GROUPS, HPG, NB])
        pcT = sb("pcT", [P, GROUPS, P])
        cmax = sb("cmax", [P, HEADS])
        csum = sb("csum", [P, HEADS])
        nmax = sb("nmax", [P, NBH])
        sums = sb("sums", [P, 2, HEADS])
        coef = sb("coef", [P, HEADS])
        keys_s = sb("keys_s", [P, 2, 4, P])
        cand = attn[:, 0:TOPK * TOPK].rearrange("p (a b) -> p a b", a=TOPK)
        onehot = atmp[:, :].rearrange("p (c k j) -> p c k j", c=2, k=TOPK)
        sv = sb("sv", [P, 2, TOPK])
        si = sb("si", [P, 2, TOPK], U32)
        sif = sb("sif", [P, 2, TOPK])
        best = sb("best", [P, TOPK])
        bi = sb("bi", [P, TOPK], U32)
        bhl = sb("bhl", [P, 2, TOPK], U32)
        bhlf = sb("bhlf", [P, 2, TOPK])
        ij = sb("ij", [P, 2, TOPK])
        bdiff = sb("bdiff", [P, TOPK])
        bexp = sb("bexp", [P, 2, TOPK])
        bsum = sb("bsum", [P, 2])
        brec = sb("brec", [P, 1])
        idx = sb("idx", [P, TILES, KTOT], U32)
        gate = sb("gate", [P, TILES * KTOT])
        ph = sb("ph", [P, 2, GRP])
        pt1 = sb("pt1", [P, GRP])
        pt2 = sb("pt2", [P, GRP])
        pt3 = sb("pt3", [P, GRP])
        pth = sb("pth", [P, 2, GRP])
        pa = sb("pa", [P, 2, GRP])
        diag = sb("diag", [P, GRP, P])

        flat = ring[:, :, :].rearrange("p a b -> p (a b)")
        xs = flat[:, 0:4096].rearrange("p (t d) -> p t d", t=TILES)
        sq_x = flat[:, 4096:5120]
        xnT = flat[:, 8192:12288].rearrange("p (c s) -> p c s", c=DC)
        kvc = flat[:, 12288:13312].rearrange("p (a s) -> p a s", a=2)
        kv2 = flat[:, 13312:15360].rearrange("p (a g s) -> p a g s", a=2, g=GROUPS)
        zc = flat[:, 0:1040].rearrange("p (a s) -> p a s", a=2)
        chs = flat[:, 1040:2064].rearrange("p (a s) -> p a s", a=2)
        cacc = flat[:, 2064:3088].rearrange("p (a s) -> p a s", a=2)
        sqc = flat[:, 5120:6144].rearrange("p (a s) -> p a s", a=2)
        cout = flat[:, 6144:7168].rearrange("p (a s) -> p a s", a=2)

        params = sem("params")
        ln1_in = sem("ln1_in")
        x_in = [sem(f"x_in{t}") for t in range(TILES)]
        xh_in = [sem(f"xh_in{i}") for i in range(2)]
        w_out_in = sem("w_out_in")
        streamed = [sem(f"streamed{i}") for i in range(SLOTS)]
        stream_used = sem("stream_used")
        consts = sem("consts")
        wide_full = [sem(f"wide_full{i}") for i in range(2)]
        wide_free = [sem(f"wide_free{i}") for i in range(2)]
        turn_full = [sem(f"turn_full{i}") for i in range(2)]
        turn_free = [sem(f"turn_free{i}") for i in range(2)]
        vorder = sem("vorder")
        xs_ready = sem("xs_ready")
        kv2_in = sem("kv2_in")
        hid_poly = sem("hid_poly")
        hid_tanh = sem("hid_tanh")
        hid_ready = sem("hid_ready")
        conv_ready = sem("conv_ready")
        ssq_done = sem("ssq_done")
        mean_done = sem("mean_done")
        cmp_shifted = sem("cmp_shifted")
        cmp_exp = sem("cmp_exp")
        max_ready = sem("max_ready")
        pv_done = sem("pv_done")
        att_free = sem("att_free")
        attn_ready = sem("attn_ready")
        keys_used = sem("keys_used")
        bdiff_ready = sem("bdiff_ready")
        bexp_ready = sem("bexp_ready")
        idx_ready = sem("idx_ready")
        landed = [sem(f"landed{i}") for i in range(RING)]
        h_ready = sem("h_ready")
        gelu_step = sem("gelu_step")
        tanh_ready = sem("tanh_ready")
        diag_ready = sem("diag_ready")
        combined = sem("combined")
        acc_read = sem("acc_read")
        out_ready = sem("out_ready")
        out_done = sem("out_done")

        N_PARAMS = 10

        def wait_full(eng, full, use):
            eng.wait_ge(full[use % 2], use // 2 + 1)

        def wait_read(eng, free, use):
            eng.wait_ge(free[use % 2], use // 2 + 1)

        def wait_free(eng, free, use):
            if use >= 2:
                eng.wait_ge(free[use % 2], use // 2)

        block = ctx.enter_context(nc.Block())

        @block.sync
        def _(sp):
            for t in range(TILES):
                sp.dma_start(xs[:, t, :], A["x"][0, t * P:(t + 1) * P, :]).then_inc(x_in[t], 16)
            sp.dma_start(ln1[:], A["ln1"]).then_inc(ln1_in, 16)

            def piece(n, src):
                if n >= SLOTS:
                    sp.wait_ge(stream_used, n - SLOTS + 1)
                sp.dma_start(stream[:, n % SLOTS, :], src).then_inc(streamed[n % SLOTS], 16)

            for n in range(SLOTS):
                piece(n, A["wpack"][n])
            for dst, name in ((pos[:], "pos"), (wg[:], "wg"), (w2k[:], "w2k"), (w2v[:], "w2v"), (convw[:], "convw"),
                              (gnc[:], "gnc"), (gna[:], "gna"), (subk[:], "subk")):
                sp.dma_start(dst, A[name]).then_inc(params, 16)
            sp.dma_start(ln2row[:], A["ln2"]).then_inc(params, 16)
            sp.dma_start(lnf[:], A["lnf"].to_broadcast([P, D])).then_inc(params, 16)
            for n in range(SLOTS, 9):
                piece(n, A["wpack"][n])
            wait_read(sp, wide_free, WIDE["kc"])
            wait_read(sp, wide_free, WIDE["vc"])
            for a in range(2):
                for g in range(GROUPS):
                    sp.dma_start(kv2[0:HD, a, g, :], kvc[g * HD:(g + 1) * HD, a, :]).then_inc(kv2_in, 16)
                    sp.dma_start(kv2[HD:P, a, g, 0:SEQ - 1], kvc[g * HD:(g + 1) * HD, a, 1:SEQ]).then_inc(kv2_in, 16)
            for n in range(9, N1):
                piece(n, A["wpack"][n])
            sp.dma_start(w_out[:], A["w_out"]).then_inc(w_out_in, 16)

            def store(t):
                sp.wait_ge(out_ready, t + 1)
                sp.dma_start(out[0, t * P:(t + 1) * P, :], xn2[:, t % 2, :]).then_inc(out_done, 16)

            for t in range(TILES):
                if t >= 2:
                    store(t - 2)
                sp.dma_start(xh[:, t % 2, :], A["x"][0, t * P:(t + 1) * P, :]).then_inc(xh_in[t % 2], 16)
                for i in range(HC):
                    piece(N1 + t * HC + i, A["wq"][i])
            for t in range(TILES - 2, TILES):
                store(t)
            sp.wait_ge(out_done, 16 * TILES)

        @block.gpsimd
        def _(pool):
            for z in (ident, causal, cmask, hidk, hidv, vbd):
                nc.gpsimd.memset(z[:], 0.0).then_inc(consts, 1)
            nc.gpsimd.memset(has_c[:], 1.0).then_inc(consts, 1)
            nc.gpsimd.memset(ones_row[:], 1.0).then_inc(consts, 1)
            nc.gpsimd.memset(mean_col[:], 1.0 / 512).then_inc(consts, 1)
            nc.gpsimd.iota(iota16i[:], pattern=[[1, TOPK]], base=0, channel_multiplier=0).then_inc(consts, 1)
            pool.wait_ge(consts, 10)
            nc.gpsimd.affine_select(out=ident[:], in_=ident[:], compare_op=ALU.not_equal, fill=1.0, base=0,
                                    pattern=[[-1, P]], channel_multiplier=1).then_inc(consts, 1)
            nc.gpsimd.affine_select(out=causal[:], in_=causal[:], compare_op=ALU.is_ge, fill=NEG, base=0,
                                    pattern=[[-1, P]], channel_multiplier=1).then_inc(consts, 1)
            nc.gpsimd.affine_select(out=cmask[:], in_=cmask[:], compare_op=ALU.is_ge, fill=NEG, base=-31,
                                    pattern=[[P, TILES], [-16, NB]], channel_multiplier=1).then_inc(consts, 1)
            nc.gpsimd.affine_select(out=has_c[:], in_=has_c[:], compare_op=ALU.is_ge, fill=0.0, base=-31,
                                    pattern=[[0, 1]], channel_multiplier=1).then_inc(consts, 1)
            nc.gpsimd.tensor_copy(iota16[:], iota16i[:]).then_inc(consts, 1)
            for t in range(TILES):
                for k in range(KTOT):
                    n = t * KTOT + k
                    if k % TOPK == 0:
                        pool.wait_ge(idx_ready, t * PH + k // TOPK + 1)
                    if n >= RING:
                        pool.wait_ge(combined, n - RING + 1)
                    nc.gpsimd.indirect_dma_start(
                        out=ring[:, n % RING, :], out_offset=None, in_=A["uv"],
                        in_offset=bass.IndirectOffsetOnAxis(ap=idx[:, t, k:k + 1], axis=0),
                    ).then_inc(landed[n % RING], 16)

        CONSTS = 15

        @block.scalar
        def _(act):
            def evac(name, dst, scale=1.0):
                use = WIDE[name]
                wait_full(act, wide_full, use)
                nc.scalar.activation(dst, wide[:, use % 2, :], ACT.Copy, scale=scale).then_inc(wide_free[use % 2], 1)

            act.wait_ge(consts, CONSTS)
            for a, name in enumerate(("kc", "vc")):
                evac(name, kvc[:, a, :])
            for a, name in enumerate(("ks", "kw")):
                evac(name, kT[:, a, :])
            for j in range(HPG):
                evac(f"q{j}", qT[:, j, :], scale=HD ** -0.5)
            for b, name in enumerate(("vs", "vw")):
                wait_full(act, wide_full, WIDE[name])
                use = WIDE[name]
                nc.scalar.activation(vtok[:, :, b, :], wide[:, use % 2, :].rearrange("p (t c) -> p t c", t=TILES),
                                     ACT.Copy).then_inc(wide_free[use % 2], 1)
            use = WIDE["gt"]
            wait_full(act, wide_full, use)
            nc.scalar.activation(sig[:, :, :, :].rearrange("p t a h -> p (t a h)"), wide[:, use % 2, 0:96], ACT.Exp,
                                 scale=-1.0).then_inc(wide_free[use % 2], 1)

            def hidden_tanh(a):
                act.wait_ge(hid_poly, a + 1)
                nc.scalar.activation(ht[:, a, :, :], ht[:, a, :, :], ACT.Tanh, scale=GELU_C).then_inc(hid_tanh, 1)

            def conv_in(c):
                if c >= 2:
                    wait_read(act, wide_free, WIDE[f"c{c - 2}"])
                evac(f"h{c}", chs[:, c % 2, :])

            def conv_out(c):
                wait_read(act, wide_free, WIDE[f"b{c}"])
                if c >= 2:
                    act.wait_ge(ssq_done, c - 1)
                nc.scalar.activation(sqc[:, c % 2, :], cout[:, c % 2, :], ACT.Square).then_inc(conv_ready, 1)
                nc.scalar.activation(convT[:, c, :], cout[:, c % 2, :], ACT.Copy,
                                     scale=gnc[:, c:c + 1]).then_inc(conv_ready, 1)

            act.wait_ge(params, 16 * N_PARAMS)
            hidden_tanh(0)
            hidden_tanh(1)
            conv_in(0)
            use = WIDE["kcc"]
            wait_full(act, wide_full, use)
            nc.scalar.activation(kcc[0:HD, :], wide[0:HD, use % 2, 0:NB], ACT.Copy)
            nc.scalar.activation(kcc[HD:P, :], wide[HD:P, use % 2, NB:2 * NB], ACT.Copy).then_inc(wide_free[use % 2], 1)
            use = WIDE["vcc"]
            wait_full(act, wide_full, use)
            for j in range(HPG):
                rows = slice(j * NB, (j + 1) * NB)
                ins = nc.scalar.activation(vbd[rows, :, j, :],
                                           wide[rows, use % 2, 0:P].rearrange("p (g d) -> p g d", g=2), ACT.Copy)
            ins.then_inc(wide_free[use % 2], 1)
            conv_out(0)
            for c in range(1, CC):
                conv_in(c)
                conv_out(c)

            def probs_exp(t, n):
                keys = (t + 1) * P
                b, h = BRANCH_HEADS[n]
                use = WIDE[("s", t, n)]
                act.wait_ge(max_ready, t * NBH + n + 1)
                if n >= 2:
                    wait_full(act, turn_full, TURN[("p", t, n - 2)])
                elif t >= 1:
                    wait_full(act, wide_full, WIDE[("pq", t - 1, 3)])
                nc.scalar.activation(probs[:, n % 2, 0:keys], wide[:, use % 2, 0:keys], ACT.Exp,
                                     bias=nmax[:, n:n + 1], accum_out=sums[:, b, h:h + 1]).then_inc(wide_free[use % 2], 1)

            def probs_turn(t, n):
                keys = (t + 1) * P
                use = TURN[("p", t, n)]
                wait_full(act, turn_full, use)
                if n >= 2:
                    act.wait_ge(pv_done, t * NBH + n - 1)
                nc.scalar.activation(probsT[:, n % 2, 0:keys], turn[:, use % 2, 0:keys],
                                     ACT.Copy).then_inc(turn_free[use % 2], 1)

            def front(name, t):
                if name == "cmp_scores":
                    act.wait_ge(cmp_shifted, t + 1)
                    nc.scalar.activation(pcs[:], pcs[:], ACT.Exp).then_inc(cmp_exp, 1)
                elif name == "cmp_out":
                    use = TURN[("pc", t)]
                    wait_full(act, turn_full, use)
                    nc.scalar.activation(pcT[:, :, :].rearrange("p g q -> p (g q)"), turn[:, use % 2, 0:2 * P],
                                         ACT.Copy).then_inc(turn_free[use % 2], 1)
                elif name.startswith("att"):
                    for n in (2 * int(name[3:]), 2 * int(name[3:]) + 1):
                        if n < NBH:
                            probs_exp(t, n)
                        if 1 <= n <= NBH:
                            probs_turn(t, n - 1)
                elif name == "norm2":
                    for i in range(2):
                        use = TURN[("x2", t, i)]
                        wait_full(act, turn_full, use)
                        nc.scalar.activation(xT2[:, i * 512:(i + 1) * 512], turn[:, use % 2, :],
                                             ACT.Copy).then_inc(turn_free[use % 2], 1)
                elif name.startswith("query"):
                    i = int(name[5:])
                    use = WIDE[("pq", t, i)]
                    wait_full(act, wide_full, use)
                    nc.scalar.activation(pq[:, i % 2, :], wide[:, use % 2, :], ACT.Copy).then_inc(wide_free[use % 2], 1)
                    use = WIDE[("ps", t, i)]
                    wait_full(act, wide_full, use)
                    m = 4 * t + i
                    if m >= 2:
                        act.wait_ge(keys_used, 2 * (m - 1))
                    nc.scalar.activation(keys_s[:, i % 2, :, :].rearrange("p a n -> p (a n)"), wide[:, use % 2, :],
                                         ACT.Copy).then_inc(wide_free[use % 2], 1)
                    if i >= 1:
                        best_exp(t, i - 1)
                elif name == "topk3":
                    best_exp(t, 3)

            def best_exp(t, i):
                for h in (2 * i, 2 * i + 1):
                    act.wait_ge(bdiff_ready, t * PH + h + 1)
                    nc.scalar.activation(bexp[:, h % 2, :], bdiff[:], ACT.Exp,
                                         accum_out=bsum[:, h % 2:h % 2 + 1]).then_inc(bexp_ready, 1)

            def peer(lo, hi):
                with nc.scalar.Fori(lo, hi) as i:
                    for q in range(2):
                        act.wait_ge(gelu_step, 10 * i + 5 * q + 3)
                        nc.scalar.activation(pth[:, q, :], pt3[:], ACT.Tanh, scale=GELU_C).then_inc(tanh_ready, 1)
                        act.wait_ge(gelu_step, 10 * i + 5 * q + 5)
                        for j in range(GRP):
                            act.wait_ge(combined, 8 * i + 4 * q + j + 1 - GRP)
                            nc.scalar.activation(diag[:, j, :], ident[:], ACT.Copy,
                                                 scale=pa[:, q, j:j + 1]).then_inc(diag_ready, 1)

            def peer_first():
                for q in range(2):
                    act.wait_ge(gelu_step, 5 * q + 3)
                    nc.scalar.activation(pth[:, q, :], pt3[:], ACT.Tanh, scale=GELU_C).then_inc(tanh_ready, 1)
                    act.wait_ge(gelu_step, 5 * q + 5)
                    for j in range(GRP):
                        if q:
                            act.wait_ge(combined, j + 1)
                        nc.scalar.activation(diag[:, j, :], ident[:], ACT.Copy,
                                             scale=pa[:, q, j:j + 1]).then_inc(diag_ready, 1)

            for name in PIECES:
                front(name, 0)
            for t in range(TILES):
                for kind, lo, hi in peer_plan(t):
                    if kind != "peer":
                        front(kind, t + 1)
                    elif lo == 0:
                        peer_first()
                        if hi > 1:
                            peer(1, hi)
                    else:
                        peer(lo, hi)

        @block.tensor
        def _(pe):
            held = [False]

            def piece(n):
                pe.wait_ge(streamed[n % SLOTS], 16 * (n // SLOTS + 1))
                return stream[:, n % SLOTS, :]

            def let_go(ins):
                if held[0]:
                    ins.then_inc(stream_used, 1)
                held[0] = False

            def transposes(name, srcs, rows=P):
                use = TURN[name]
                wait_free(pe, turn_free, use)
                for i, s in enumerate(srcs):
                    ins = nc.tensor.transpose(turn[:, use % 2, i * P:(i + 1) * P], s, ident[:])
                ins.then_inc(turn_full[use % 2], 1)

            pe.wait_ge(consts, CONSTS)
            for t in range(TILES):
                pe.wait_ge(xs_ready, t + 1)
                for i in range(2):
                    transposes(("x", t, i), [xs[:, t, (4 * i + c) * P:(4 * i + c + 1) * P] for c in range(4)])
            for i in range(2):
                pe.wait_ge(turn_free[i], TILES)
            def channels(name):
                w = piece(STREAM1.index(name)).rearrange("p (c n) -> p c n", c=DC)
                use = WIDE[name]
                wait_free(pe, wide_free, use)
                for c in range(DC):
                    ins = nc.tensor.matmul(wide[:, use % 2, :], w[:, c, :], xnT[:, c, :], start=(c == 0),
                                           stop=(c == DC - 1))
                    if c == 0:
                        let_go(ins)
                ins.then_inc(wide_full[use % 2], 1)
                held[0] = True

            def tokens(name, w, cols):
                use = WIDE[name]
                wait_free(pe, wide_free, use)
                for t in range(TILES):
                    for c in range(DC):
                        ins = nc.tensor.matmul(wide[:, use % 2, t * cols:(t + 1) * cols],
                                               xnT[:, c, t * P:(t + 1) * P], w[:, c, :],
                                               start=(c == 0), stop=(c == DC - 1))
                        let_go(ins)
                ins.then_inc(wide_full[use % 2], 1)

            for name in ("kc", "vc", "ks", "kw", "q0", "q1", "q2", "q3"):
                channels(name)
            for name in ("vs", "vw"):
                tokens(name, piece(STREAM1.index(name)).rearrange("p (c n) -> p c n", c=DC), P)
                held[0] = True
            pe.wait_ge(params, 16 * N_PARAMS)
            tokens("gt", wg, 24)

            def hidden(a):
                name = "kv"[a]
                use = WIDE[f"hid{name}"]
                wait_free(pe, wide_free, use)
                if a == 0:
                    pe.wait_ge(kv2_in, 16 * 8)
                o = wide[:, use % 2, :]
                for m in range(LPAIRS):
                    if m % 4 == 0:
                        w = piece(STREAM1.index(f"w1{name}{m // 4}")).rearrange("p (m n) -> p m n", m=4)
                    for hh in range(2):
                        lhs = w[:, m % 4, hh * P:(hh + 1) * P]
                        blocks = kv2[:, a, :, 2 * m:2 * m + 16 * (NCMP - 1) + 1:16]
                        ins = nc.tensor.matmul(o[:, hh * 64:hh * 64 + 62].rearrange("p (g n) -> p g n", g=2), lhs, blocks,
                                               start=(m == 0 and hh == 0), stop=(m == LPAIRS - 1),
                                               skip_group_check=True)
                        let_go(ins)
                        ins = nc.tensor.matmul(o[:, hh * 64 + 62:hh * 64 + 63], lhs, pos[:, a, m:m + 1],
                                               start=False, stop=(m == LPAIRS - 1), skip_group_check=True)
                    held[0] = m % 4 == 3
                ins.then_inc(wide_full[use % 2], 1)

            hidden(0)
            hidden(1)

            def conv(c):
                for s in "hcb":
                    channels(f"{s}{c}")

            def conv_squares(c):
                pe.wait_ge(conv_ready, 2 * c + 1)
                for t in range(TILES):
                    ins = nc.tensor.matmul(att_ps[:, 0, t:t + 1], sqc[:, c % 2, t * P:(t + 1) * P], mean_col[:],
                                           start=(c == 0 and t == 0), stop=(c == CC - 1), skip_group_check=True)
                    let_go(ins)
                ins.then_inc(ssq_done, 1)

            conv(0)
            pe.wait_ge(hid_ready, 2)
            use = WIDE["kcc"]
            wait_free(pe, wide_free, use)
            for hh in range(2):
                ins = nc.tensor.matmul(wide[:, use % 2, 0:2 * NB], w2k[:, hh, :],
                                       hidk[:, hh, :, :].rearrange("p g n -> p (g n)"), start=(hh == 0), stop=(hh == 1))
            ins.then_inc(wide_full[use % 2], 1)
            use = WIDE["vcc"]
            wait_free(pe, wide_free, use)
            for g in range(GROUPS):
                for hh in range(2):
                    ins = nc.tensor.matmul(wide[:, use % 2, g * HD:(g + 1) * HD],
                                           hidv[:, hh, g, :, :].rearrange("p j n -> p (j n)"), w2v[:, hh, :],
                                           start=(hh == 0), stop=(hh == 1))
            ins.then_inc(wide_full[use % 2], 1)
            for c in range(1, CC):
                conv(c)
                conv_squares(c - 1)
            conv_squares(CC - 1)

            def scores(t, n):
                b, h = BRANCH_HEADS[n]
                g, j = h // HPG, h % HPG
                rows = slice(g * HD, (g + 1) * HD)
                use = WIDE[("s", t, n)]
                wait_free(pe, wide_free, use)
                nc.tensor.matmul(wide[:, use % 2, 0:(t + 1) * P], qT[rows, j, t * P:(t + 1) * P],
                                 kT[rows, b, 0:(t + 1) * P], start=True, stop=True).then_inc(wide_full[use % 2], 1)

            def values(t, n):
                b, h = BRANCH_HEADS[n]
                use = TURN[("p", t, n)]
                wait_read(pe, turn_free, use)
                if n % HEADS == 0:
                    if t >= 1:
                        pe.wait_ge(att_free, 2 * (t - 1) + b + 1)
                    elif b == 0:
                        pe.wait_ge(mean_done, 1)
                for kb in range(t + 1):
                    ins = nc.tensor.matmul(att_ps[:, b, h * HD:(h + 1) * HD], probsT[:, n % 2, kb * P:(kb + 1) * P],
                                           vtok[:, kb, b, (h // HPG) * HD:(h // HPG + 1) * HD],
                                           start=(kb == 0), stop=(kb == t))
                ins.then_inc(pv_done, 1)

            def front(name, t):
                if name == "cmp_scores":
                    if t == 0:
                        wait_read(pe, wide_free, WIDE["kcc"])
                    for g in range(GROUPS):
                        use = WIDE[("sc", t, g)]
                        wait_free(pe, wide_free, use)
                        rows = slice(g * HD, (g + 1) * HD)
                        for j in range(HPG):
                            ins = nc.tensor.matmul(wide[:, use % 2, j * NB:(j + 1) * NB], qT[rows, j, t * P:(t + 1) * P],
                                                   kcc[rows, :], start=True, stop=True)
                        ins.then_inc(wide_full[use % 2], 1)
                elif name == "cmp_out":
                    pe.wait_ge(cmp_exp, t + 1)
                    transposes(("pc", t), [pcs[:, g, :, :].rearrange("p j n -> p (j n)") for g in range(GROUPS)])
                    wait_read(pe, turn_free, TURN[("pc", t)])
                    if t == 0:
                        wait_read(pe, wide_free, WIDE["vcc"])
                    use = WIDE[("oc", t)]
                    wait_free(pe, wide_free, use)
                    for g in range(GROUPS):
                        ins = nc.tensor.matmul(wide[:, use % 2, g * 256:(g + 1) * 256], pcT[:, g, :],
                                               vbd[:, g, :, :].rearrange("p j d -> p (j d)"), start=True, stop=True)
                    ins.then_inc(wide_full[use % 2], 1)
                elif name.startswith("att"):
                    for n in (2 * int(name[3:]), 2 * int(name[3:]) + 1):
                        if n < NBH:
                            scores(t, n)
                        if 1 <= n <= NBH:
                            wait_read(pe, wide_free, WIDE[("s", t, n - 1)])
                            transposes(("p", t, n - 1), [probs[:, (n - 1) % 2, kb * P:(kb + 1) * P]
                                                         for kb in range(t + 1)])
                        if 2 <= n:
                            values(t, n - 2)
                elif name == "mix":
                    pe.wait_ge(attn_ready, t + 1)
                    transposes(("at", t), [attn[:, c * P:(c + 1) * P] for c in range(CC)])
                    if t == 0:
                        pe.wait_ge(w_out_in, 16)
                        pe.wait_ge(conv_ready, 2 * CC)
                    for half in range(2):
                        cols = slice(half * 512, (half + 1) * 512)
                        use = WIDE[("yc", t, half)]
                        wait_free(pe, wide_free, use)
                        for c in range(CC):
                            ins = nc.tensor.matmul(wide[:, use % 2, :], convT[:, c, t * P:(t + 1) * P],
                                                   w_out[:, c, cols], start=(c == 0), stop=(c == CC - 1))
                        ins.then_inc(wide_full[use % 2], 1)
                        if half == 0:
                            wait_read(pe, turn_free, TURN[("at", t)])
                        use = WIDE[("ya", t, half)]
                        wait_free(pe, wide_free, use)
                        for c in range(CC):
                            ins = nc.tensor.matmul(wide[:, use % 2, :], attT[:, c * P:(c + 1) * P],
                                                   w_out[:, CC + c, cols], start=(c == 0), stop=(c == CC - 1))
                        ins.then_inc(wide_full[use % 2], 1)
                elif name == "norm2":
                    for half in range(2):
                        use = WIDE[("g2", t, half)]
                        wait_free(pe, wide_free, use)
                        nc.tensor.matmul(wide[:, use % 2, :], ones_row[:], ln2row[:, half * 512:(half + 1) * 512],
                                         start=True, stop=True).then_inc(wide_full[use % 2], 1)
                    for i in range(2):
                        wait_read(pe, wide_free, WIDE[("g2", t, i)])
                        transposes(("x2", t, i), [xn2[:, t % 2, (4 * i + c) * P:(4 * i + c + 1) * P] for c in range(4)])
                elif name.startswith("query"):
                    i = int(name[5:])
                    if i == 0:
                        for k in range(2):
                            wait_read(pe, turn_free, TURN[("x2", t, k)])
                    use = WIDE[("pq", t, i)]
                    wait_free(pe, wide_free, use)
                    for a in range(4):
                        w = piece(N1 + t * HC + 4 * i + a).rearrange("p (c n) -> p c n", c=DC)
                        for c in range(DC):
                            ins = nc.tensor.matmul(wide[:, use % 2, a * P:(a + 1) * P], w[:, c, :],
                                                   xT2[:, c * P:(c + 1) * P], start=(c == 0), stop=(c == DC - 1))
                            let_go(ins)
                        held[0] = True
                    ins.then_inc(wide_full[use % 2], 1)
                    wait_read(pe, wide_free, use)
                    use = WIDE[("ps", t, i)]
                    wait_free(pe, wide_free, use)
                    for a in range(4):
                        ins = nc.tensor.matmul(wide[:, use % 2, a * P:(a + 1) * P], pq[:, i % 2, a * P:(a + 1) * P],
                                               subk[:, 4 * i + a, :], start=True, stop=True)
                        let_go(ins)
                    ins.then_inc(wide_full[use % 2], 1)

            def combine(i, j, first=False, last=False):
                pe.wait_ge(diag_ready, 8 * i + j + 1)
                for half in range(2):
                    ins = nc.tensor.matmul(acc[:, half, :], diag[:, j % GRP, :],
                                           ring[:, j, D + half * 512:D + (half + 1) * 512],
                                           start=first, stop=last, skip_group_check=True)
                ins.then_inc(combined, 1)

            def peer(lo, hi):
                if lo % ITERS == 0:
                    if lo:
                        pe.wait_ge(acc_read, 2 * (lo // ITERS))
                    for j in range(RING):
                        combine(lo, j, first=(j == 0))
                    lo += 1
                end = hi - 1 if hi % ITERS == 0 else hi
                if lo < end:
                    with nc.tensor.Fori(lo, end) as i:
                        for j in range(RING):
                            combine(i, j)
                if end < hi:
                    for j in range(RING):
                        combine(end, j, last=(j == RING - 1))

            for name in PIECES:
                front(name, 0)
            for t in range(TILES):
                for kind, lo, hi in peer_plan(t):
                    if kind == "peer":
                        peer(lo, hi)
                    else:
                        front(kind, t + 1)

        @block.vector
        def _(dve):
            v = nc.vector
            count = [0]

            def then(ins):
                count[0] += 1
                ins.then_inc(vorder, 1)
                dve.wait_ge(vorder, count[0])

            def bcast(ap, n):
                return ap.unsqueeze(2).to_broadcast([ap.shape[0], ap.shape[1], n])

            def rstd(dst, mean, last=None):
                n = dst.shape[1]
                x, y, e = (newton[:, k, 0:n] for k in range(3))
                then(v.tensor_scalar(x, mean, EPS, None, ALU.add))
                then(v.tensor_scalar(y.bitcast(U32), x.bitcast(U32), -0.5, float(0x5F3759DF), ALU.mult, ALU.add))
                for step in range(3):
                    then(v.tensor_tensor(e, y, y, ALU.mult))
                    then(v.tensor_tensor(e, e, x, ALU.mult))
                    then(v.tensor_scalar(e, e, -0.5, 1.5, ALU.mult, ALU.add))
                    ins = v.tensor_tensor(dst if step == 2 else y, y, e, ALU.mult)
                    if step == 2 and last is not None:
                        ins.then_inc(last, 1)
                    else:
                        then(ins)

            dve.wait_ge(consts, CONSTS)
            for t in range(TILES):
                dve.wait_ge(x_in[t], 16)
                then(v.tensor_tensor_reduce(sq_x, xs[:, t, :], xs[:, t, :], 1.0 / D, 0.0, ALU.mult, ALU.add,
                                            stat[:, 0:1]))
                rstd(stat[:, 1:2], stat[:, 0:1])
                v.tensor_scalar(xs[:, t, :], xs[:, t, :], stat[:, 1:2], None, ALU.mult).then_inc(xs_ready, 1)
                if t == 0:
                    dve.wait_ge(ln1_in, 16)
                for i in range(2):
                    use = TURN[("x", t, i)]
                    wait_full(dve, turn_full, use)
                    v.tensor_tensor(xnT[:, 4 * i:4 * i + 4, t * P:(t + 1) * P],
                                    turn[:, use % 2, :].rearrange("p (c q) -> p c q", c=4),
                                    bcast(ln1[:, 4 * i:4 * i + 4], P), ALU.mult).then_inc(turn_free[use % 2], 1)
            then(v.memset(zc[:, :, 0:2], 0.0))

            dve.wait_ge(params, 16 * N_PARAMS)
            use = WIDE["gt"]
            wait_read(dve, wide_free, use)
            sg = sig[:, :, :, :].rearrange("p t a h -> p (t a h)")
            then(v.tensor_scalar(sg, sg, 1.0, None, ALU.add))
            then(v.reciprocal(sg, sg))

            def hidden(a):
                use = WIDE["hid" + "kv"[a]]
                wait_full(dve, wide_full, use)
                o = wide[:, use % 2, 0:P].rearrange("p (h n) -> p h n", h=2)
                then(v.tensor_copy(hbias[:, a, :], o[:, :, 62]))
                for hh in range(2):
                    then(v.tensor_scalar(hx[:, a, hh, :], o[:, hh, 0:62], hbias[:, a, hh:hh + 1], None, ALU.add))
                hxa, hta = (z[:, a, :, :].rearrange("p h n -> p (h n)") for z in (hx, ht))
                ins = v.tensor_tensor(hta, hxa, hxa, ALU.mult)
                ins.then_inc(wide_free[use % 2], 1)
                wait_read(dve, wide_free, use)
                then(v.tensor_scalar(hta, hta, 0.044715, 1.0, ALU.mult, ALU.add))
                v.tensor_tensor(hta, hta, hxa, ALU.mult).then_inc(hid_poly, 1)

            def hidden_out(a):
                dve.wait_ge(hid_tanh, a + 1)
                hxa, hta = (z[:, a, :, :].rearrange("p h n -> p (h n)") for z in (hx, ht))
                then(v.scalar_tensor_tensor(hta, hta, 1.0, hxa, ALU.add, ALU.mult))
                for hh in range(2):
                    src = ht[:, a, hh, :].rearrange("p (g n) -> p g n", g=2)
                    if a == 0:
                        ins = v.tensor_scalar(hidk[:, hh, :, 0:NCMP], src, 0.5, None, ALU.mult)
                    else:
                        for j in range(HPG):
                            ins = v.tensor_scalar(hidv[:, hh, :, j, 0:NCMP], src, 0.5, None, ALU.mult)
                ins.then_inc(hid_ready, 1)

            hidden(0)
            hidden(1)
            hidden_out(0)
            hidden_out(1)

            for c in range(CC):
                b = c % 2
                use = WIDE[f"h{c}"]
                wait_read(dve, wide_free, use)
                use = WIDE[f"c{c}"]
                wait_full(dve, wide_full, use)
                v.tensor_tensor(zc[:, b, 2:514], chs[:, b, :], wide[:, use % 2, :],
                                ALU.mult).then_inc(wide_free[use % 2], 1)
                wait_read(dve, wide_free, use)
                then(v.tensor_scalar(cacc[:, b, :], zc[:, b, 0:512], convw[:, c, 0:1], None, ALU.mult))
                for k in (1, 2):
                    then(v.scalar_tensor_tensor(cacc[:, b, :], zc[:, b, k:k + 512], convw[:, c, k:k + 1],
                                                cacc[:, b, :], ALU.mult, ALU.add))
                use = WIDE[f"b{c}"]
                wait_full(dve, wide_full, use)
                if c >= 2:
                    dve.wait_ge(conv_ready, 2 * (c - 1))
                v.tensor_tensor(cout[:, b, :], cacc[:, b, :], wide[:, use % 2, :],
                                ALU.mult).then_inc(wide_free[use % 2], 1)
            dve.wait_ge(ssq_done, CC)
            then(v.tensor_copy(rstd_c[:], att_ps[:, 0, 0:TILES]))
            rstd(rstd_c[:], rstd_c[:], mean_done)

            def branch_out(t, b):
                dve.wait_ge(pv_done, t * NBH + HEADS * (b + 1))
                then(v.reciprocal(coef[:], sums[:, b, :]))
                then(v.tensor_tensor(coef[:], coef[:], sig[:, t, 1 + b, :], ALU.mult))
                then(v.tensor_tensor(atmp[:, :].rearrange("p (h d) -> p h d", h=HEADS),
                                     att_ps[:, b, :].rearrange("p (h d) -> p h d", h=HEADS), bcast(coef[:], HD),
                                     ALU.mult))
                v.tensor_tensor(attn[:], attn[:], atmp[:], ALU.add).then_inc(att_free, 1)
                dve.wait_ge(att_free, 2 * t + b + 1)

            def row_max(t, n):
                use = WIDE[("s", t, n)]
                wait_full(dve, wide_full, use)
                own = wide[:, use % 2, t * P:(t + 1) * P]
                then(v.tensor_tensor(own, own, causal[:], ALU.add))
                if n == 0 and t >= 1:
                    wait_read(dve, wide_free, WIDE[("s", t - 1, NBH - 1)])
                v.tensor_reduce(nmax[:, n:n + 1], wide[:, use % 2, 0:(t + 1) * P], AX_X, ALU.max,
                                negate=True).then_inc(max_ready, 1)

            def top16(src, vals, inds):
                then(v.max(vals[:, 0:8], src))
                then(v.max_index(inds[:, 0:8], vals[:, 0:8], src))
                then(v.match_replace(src, vals[:, 0:8], src, -3.0e38))
                then(v.max(vals[:, 8:16], src))
                then(v.max_index(inds[:, 8:16], vals[:, 8:16], src))

            def topk(t, i):
                use = WIDE[("ps", t, i)]
                wait_read(dve, wide_free, use)
                for hh in range(2):
                    h = 2 * i + hh
                    for c in range(2):
                        top16(keys_s[:, i % 2, 2 * hh + c, :], sv[:, c, :], si[:, c, :])
                    v.tensor_tensor(cand, bcast(sv[:, 0, :], TOPK), sv[:, 1:2, :].to_broadcast([P, TOPK, TOPK]),
                                    ALU.add).then_inc(keys_used, 1)
                    dve.wait_ge(keys_used, t * PH + h + 1)
                    top16(cand.rearrange("p a b -> p (a b)"), best, bi)
                    m = t * PH + h
                    if m >= 1:
                        dve.wait_ge(bexp_ready, m)
                    v.tensor_scalar(bdiff[:], best[:], best[:, 0:1], None, ALU.subtract).then_inc(bdiff_ready, 1)
                    then(v.tensor_scalar(bhl[:, 0, :], bi[:], 4, None, ALU.logical_shift_right))
                    then(v.tensor_scalar(bhl[:, 1, :], bi[:], 15, None, ALU.bitwise_and))
                    then(v.tensor_copy(bhlf[:], bhl[:]))
                    then(v.tensor_copy(sif[:], si[:]))
                    oh = onehot.rearrange("p c k j -> p (c k) j")
                    then(v.tensor_tensor(oh, bcast(bhlf[:, :, :].rearrange("p c k -> p (c k)"), TOPK),
                                         iota16[:].unsqueeze(1).to_broadcast([P, 2 * TOPK, TOPK]), ALU.is_equal))
                    then(v.tensor_tensor(onehot, onehot, sif[:].unsqueeze(2).to_broadcast([P, 2, TOPK, TOPK]),
                                         ALU.mult))
                    then(v.tensor_reduce(ij[:, :, :].rearrange("p c k -> p (c k)"), oh, AX_X, ALU.add))
                    v.scalar_tensor_tensor(idx[:, t, h * TOPK:(h + 1) * TOPK], ij[:, 0, :], float(P), ij[:, 1, :],
                                           ALU.mult, ALU.add).then_inc(idx_ready, 1)
                    dve.wait_ge(bexp_ready, m + 1)
                    then(v.reciprocal(brec[:], bsum[:, h % 2:h % 2 + 1]))
                    then(v.tensor_scalar(gate[:, m * TOPK:(m + 1) * TOPK], bexp[:, h % 2, :], brec[:], 0.5, ALU.mult,
                                         ALU.mult))

            def front(name, t):
                if name == "cmp_scores":
                    for g in range(GROUPS):
                        use = WIDE[("sc", t, g)]
                        wait_full(dve, wide_full, use)
                        v.tensor_tensor(pcs[:, g, :, :], wide[:, use % 2, 0:P].rearrange("p (j n) -> p j n", j=HPG),
                                        cmask[:, t:t + 1, :].to_broadcast([P, HPG, NB]),
                                        ALU.add).then_inc(wide_free[use % 2], 1)
                        wait_read(dve, wide_free, use)
                    heads = pcs[:, :, :, :].rearrange("p g j n -> p (g j) n")
                    then(v.tensor_reduce(cmax[:], heads, AX_X, ALU.max))
                    v.tensor_tensor(heads, heads, bcast(cmax[:], NB), ALU.subtract).then_inc(cmp_shifted, 1)
                elif name == "cmp_out":
                    dve.wait_ge(cmp_exp, t + 1)
                    then(v.tensor_reduce(csum[:], pcs[:, :, :, :].rearrange("p g j n -> p (g j) n"), AX_X, ALU.add))
                    then(v.reciprocal(coef[:], csum[:]))
                    then(v.tensor_tensor(coef[:], coef[:], sig[:, t, 0, :], ALU.mult))
                    if t == 0:
                        then(v.tensor_scalar(coef[:], coef[:], has_c[:], None, ALU.mult))
                    use = WIDE[("oc", t)]
                    wait_full(dve, wide_full, use)
                    v.tensor_tensor(attn[:, :].rearrange("p (h d) -> p h d", h=HEADS),
                                    wide[:, use % 2, :].rearrange("p (h d) -> p h d", h=HEADS), bcast(coef[:], HD),
                                    ALU.mult).then_inc(wide_free[use % 2], 1)
                    wait_read(dve, wide_free, use)
                elif name.startswith("att"):
                    for n in (2 * int(name[3:]), 2 * int(name[3:]) + 1):
                        if n < NBH:
                            row_max(t, n)
                        if n == HEADS + 2:
                            branch_out(t, 0)
                    if n >= NBH:
                        branch_out(t, 1)
                elif name == "mix":
                    then(v.tensor_tensor_reduce(atmp[:], attn[:], attn[:], 1.0 / 512, 0.0, ALU.mult, ALU.add,
                                                stat[:, 0:1]))
                    rstd(stat[:, 1:2], stat[:, 0:1])
                    v.tensor_scalar(attn[:], attn[:], stat[:, 1:2], None, ALU.mult).then_inc(attn_ready, 1)
                    use = TURN[("at", t)]
                    wait_full(dve, turn_full, use)
                    v.tensor_tensor(attT[:, :].rearrange("p (c q) -> p c q", c=CC),
                                    turn[:, use % 2, :].rearrange("p (c q) -> p c q", c=CC), bcast(gna[:], P),
                                    ALU.mult).then_inc(turn_free[use % 2], 1)
                    dve.wait_ge(xh_in[t % 2], 16 * (t // 2 + 1))
                    for half in range(2):
                        xhh = xh[:, t % 2, half * 512:(half + 1) * 512]
                        use = WIDE[("yc", t, half)]
                        wait_full(dve, wide_full, use)
                        v.scalar_tensor_tensor(xhh, wide[:, use % 2, :], rstd_c[:, t:t + 1], xhh, ALU.mult,
                                               ALU.add).then_inc(wide_free[use % 2], 1)
                        wait_read(dve, wide_free, use)
                        use = WIDE[("ya", t, half)]
                        wait_full(dve, wide_full, use)
                        v.tensor_tensor(xhh, xhh, wide[:, use % 2, :], ALU.add).then_inc(wide_free[use % 2], 1)
                        wait_read(dve, wide_free, use)
                elif name == "norm2":
                    h1 = xh[:, t % 2, :]
                    if t >= 2:
                        dve.wait_ge(out_done, 16 * (t - 1))
                    then(v.tensor_tensor_reduce(xn2[:, t % 2, :], h1, h1, 1.0 / D, 0.0, ALU.mult, ALU.add, stat[:, 0:1]))
                    rstd(stat[:, 1:2], stat[:, 0:1])
                    for half in range(2):
                        cols = slice(half * 512, (half + 1) * 512)
                        use = WIDE[("g2", t, half)]
                        wait_full(dve, wide_full, use)
                        v.scalar_tensor_tensor(xn2[:, t % 2, cols], xh[:, t % 2, cols], stat[:, 1:2],
                                               wide[:, use % 2, :], ALU.mult, ALU.mult).then_inc(wide_free[use % 2], 1)
                        wait_read(dve, wide_free, use)
                elif name.startswith("query"):
                    if int(name[5:]) >= 1:
                        topk(t, int(name[5:]) - 1)
                elif name == "topk3":
                    topk(t, 3)

            def peer(lo, hi, t):
                xt = xn2[:, t % 2, :]
                with nc.vector.Fori(lo, hi) as i:
                    for q in range(2):
                        for j in range(GRP):
                            s = q * GRP + j
                            dve.wait_ge(landed[s], 16 * i + 16)
                            v.tensor_tensor_reduce(ring[:, s, 0:D], ring[:, s, 0:D], xt, 1.0, 0.0, ALU.mult, ALU.add,
                                                   ph[:, q, j:j + 1]).then_inc(h_ready, 1)
                        dve.wait_ge(h_ready, 8 * i + 4 * q + 4)
                        v.tensor_tensor(pt1[:], ph[:, q, :], ph[:, q, :], ALU.mult).then_inc(gelu_step, 1)
                        dve.wait_ge(gelu_step, 10 * i + 5 * q + 1)
                        v.tensor_scalar(pt2[:], pt1[:], 0.044715, 1.0, ALU.mult, ALU.add).then_inc(gelu_step, 1)
                        dve.wait_ge(gelu_step, 10 * i + 5 * q + 2)
                        v.tensor_tensor(pt3[:], pt2[:], ph[:, q, :], ALU.mult).then_inc(gelu_step, 1)
                        dve.wait_ge(tanh_ready, 2 * i + q + 1)
                        v.scalar_tensor_tensor(pt2[:], pth[:, q, :], 1.0, ph[:, q, :], ALU.add,
                                               ALU.mult).then_inc(gelu_step, 1)
                        dve.wait_ge(gelu_step, 10 * i + 5 * q + 4)
                        v.tensor_tensor(pa[:, q, :], pt2[:], gate[:, bass.ds(i * RING + q * GRP, GRP)],
                                        ALU.mult).then_inc(gelu_step, 1)

            def finish(t):
                h1 = xh[:, t % 2, :]
                dve.wait_ge(combined, (t + 1) * KTOT)
                for half in range(2):
                    cols = slice(half * 512, (half + 1) * 512)
                    v.tensor_tensor(xh[:, t % 2, cols], xh[:, t % 2, cols], acc[:, half, :],
                                    ALU.add).then_inc(acc_read, 1)
                dve.wait_ge(acc_read, 2 * (t + 1))
                then(v.tensor_tensor_reduce(xn2[:, t % 2, :], h1, h1, 1.0 / D, 0.0, ALU.mult, ALU.add, stat[:, 2:3]))
                rstd(stat[:, 2:3], stat[:, 2:3])
                v.scalar_tensor_tensor(xn2[:, t % 2, :], h1, stat[:, 2:3], lnf[:], ALU.mult,
                                       ALU.mult).then_inc(out_ready, 1)

            for name in PIECES:
                front(name, 0)
            for t in range(TILES):
                for kind, lo, hi in peer_plan(t):
                    if kind == "peer":
                        peer(lo, hi, t)
                    else:
                        front(kind, t + 1)
                finish(t)


def peer_plan(t):
    base = t * ITERS
    if t == TILES - 1:
        return [("peer", base, base + ITERS)]
    plan, at = [], 0
    gaps = ITERS - 2
    for p, name in enumerate(PIECES):
        to = 1 + p * gaps // len(PIECES)
        if to > at:
            plan.append(("peer", base + at, base + to))
            at = to
        plan.append((name, 0, 0))
    plan.append(("peer", base + at, base + ITERS))
    return plan


def kernel(x, ln1, w_in, conv_w, cmp_pos_k, cmp_pos_v, cmp_k_w1, cmp_k_w2, cmp_v_w1, cmp_v_w2,
           gn_conv, gn_attn, w_out, ln2, peer_wq, peer_subkeys, peer_u, peer_v, ln_f):
    import concourse.bacc as bacc
    from concourse.bass_utils import run_bass_kernel_spmd

    col = {}
    at = 0
    for name, n in (("h", 512), ("b", 512), ("c", 512), ("q", 512), ("kc", 128), ("vc", 128), ("ks", 128), ("vs", 128),
                    ("kw", 128), ("vw", 128), ("g", 24)):
        col[name] = w_in[0][:, at:at + n]
        at += n

    def rows(w):
        return np.asarray(w).reshape(-1, P, w.shape[1]).transpose(1, 0, 2)

    def pack(name):
        if name[:2] in ("kc", "vc", "ks", "kw", "vs", "vw"):
            return rows(col[name])
        if name[0] == "q":
            j = int(name[1])
            w = np.asarray(col["q"]).reshape(D, GROUPS, HPG, HD)[:, :, j, :].reshape(D, P)
            return rows(w)
        if name[:2] == "w1":
            w = (cmp_k_w1 if name[2] == "k" else cmp_v_w1)[0]
            return rows(w)[:, 4 * int(name[3]):4 * int(name[3]) + 4, :]
        c = int(name[1])
        return rows(col[name[0]][:, c * P:(c + 1) * P])

    def columns(a):
        return np.asarray(a).reshape(-1, P).T

    arrays = {
        "x": x,
        "ln1": columns(ln1[0]),
        "wpack": np.stack([pack(n).reshape(P, D) for n in STREAM1]),
        "pos": np.stack([np.asarray(p[0]).reshape(LPAIRS, P).T for p in (cmp_pos_k, cmp_pos_v)], axis=1),
        "wg": rows(np.asarray(col["g"]).reshape(D, HEADS, 3).transpose(0, 2, 1).reshape(D, 24)),
        "w2k": rows(np.concatenate([cmp_k_w2[0], cmp_k_w2[0]], axis=1)),
        "w2v": rows(cmp_v_w2[0]),
        "convw": np.asarray(conv_w[0]).reshape(3, CC, P).transpose(2, 1, 0),
        "gnc": columns(gn_conv[0]),
        "gna": columns(gn_attn[0]),
        "subk": np.asarray(peer_subkeys[0]).reshape(HC, P, P).transpose(2, 0, 1),
        "ln2": np.asarray(ln2),
        "lnf": np.asarray(ln_f)[None, :],
        "w_out": rows(w_out[0]),
        "wq": np.asarray(peer_wq[0]).reshape(DC, P, HC, P).transpose(2, 1, 0, 3).reshape(HC, P, D),
        "uv": np.concatenate([peer_u[0], peer_v[0]], axis=1),
    }
    arrays = {name: np.ascontiguousarray(a) for name, a in arrays.items()}
    nc = bacc.Bacc("TRN2", target_bir_lowering=False, num_devices=1)
    aps = {name: nc.dram_tensor(name + "_dram", a.shape, mybir.dt.from_np(a.dtype), kind="ExternalInput").ap()
           for name, a in arrays.items()}
    out = nc.dram_tensor("out_dram", (1, SEQ, D), F32, kind="ExternalOutput").ap()
    layer(nc, aps, out)
    r = run_bass_kernel_spmd(nc, [{name + "_dram": a for name, a in arrays.items()}], core_ids=[0])
    return r.results[0]["out_dram"]
```

```python
from contextlib import ExitStack

import numpy as np

import concourse.bass as bass
from concourse import mybir

F32 = mybir.dt.float32
U32 = mybir.dt.uint32
ALU = mybir.AluOpType
ACT = mybir.ActivationFunctionType
AX_X = mybir.AxisListType.X

P = 128
SEQ, D = 512, 1024
TILES = SEQ // P
DC = D // P
HEADS, GROUPS, HD = 8, 2, 64
HPG = HEADS // GROUPS
NB = 32
NCMP = (SEQ - 32) // 16 + 1
LPAIRS = 16
CC = 4
PH = 8
HC = 2 * PH
TOPK = 16
KTOT = PH * TOPK
EPS = 1e-6
NEG = -1e30
GELU_C = float(np.sqrt(2.0 / np.pi))
RING = 8
GRP = 4
GPE = 3
ITERS = KTOT // RING
SLOTS = 4

STREAM1 = (["kc", "vc", "ks", "kw", "q0", "q1", "q2", "q3", "vs", "vw"]
           + [f"w1k{i}" for i in range(4)] + [f"w1v{i}" for i in range(4)]
           + [f"{s}{c}" for c in range(CC) for s in "hcb"])
N1 = len(STREAM1)

BRANCH_HEADS = [(b, h) for b in range(2) for h in (0, 4, 1, 5, 2, 6, 3, 7)]
NBH = len(BRANCH_HEADS)

GAPS = 2 * ITERS - 1


def front_plan():
    plan = [{"pe": [], "act": [], "dve": []} for _ in range(GAPS)]

    def put(gap, engine, *step):
        plan[gap][engine].append(step)

    put(0, "pe", "cmp_scores")
    put(1, "dve", "cmp_shift")
    put(1, "act", "cmp_exp")
    put(1, "pe", "cmp_turn")
    put(2, "dve", "cmp_coef")
    put(2, "act", "cmp_turned")
    put(2, "pe", "cmp_values")
    put(3, "dve", "cmp_out")
    pairs = NBH // 2
    for gap in range(3, 3 + pairs + 2):
        two = lambda pair: (2 * pair, 2 * pair + 1) if 0 <= pair < pairs else ()
        for n in two(gap - 4):
            put(gap, "dve", "max", n)
        for n in two(gap - 5):
            put(gap, "act", "turned", n)
            put(gap, "pe", "values", n)
        for n in two(gap - 4):
            put(gap, "act", "exp", n)
            put(gap, "pe", "turn", n)
        for n in two(gap - 3):
            put(gap, "pe", "scores", n)
    put(5 + pairs // 2, "dve", "branch", 0)
    put(12, "pe", "yc", 0)
    put(12, "pe", "yc", 1)
    put(13, "dve", "branch", 1)
    put(13, "dve", "att_norm")
    put(13, "pe", "att_turn")
    put(13, "dve", "add_yc", 0)
    put(13, "dve", "add_yc", 1)
    put(14, "dve", "att_turned")
    put(14, "pe", "ya", 0)
    put(14, "pe", "ya", 1)
    put(15, "dve", "norm2")
    put(15, "pe", "x2_turn")
    put(16, "act", "x2_turned")
    for i, (gap_pq, gap_ps, gap_out) in enumerate(((16, 17, 18), (17, 18, 19), (18, 20, 21), (19, 22, 24))):
        put(gap_ps, "act", "pq_out", i)
        put(gap_out, "act", "ps_out", i)
    for gap, names in ((16, ["pq0"]), (17, ["ps0", "pq1"]), (18, ["ps1", "pq2"]), (20, ["ps2", "pq3"]), (22, ["ps3"])):
        for name in names:
            put(gap, "pe", name[:2], int(name[2]))
    for n in range(3 * PH):
        gap, h = 19 + n // 2, n // 3
        put(gap, "dve", ("keys", "cand", "place")[n % 3], h)
        if n % 3 == 1:
            put(gap, "act", "best_exp", h)
        if n % 3 == 0 and h:
            put(gap, "dve", "gates", h - 1)
    put(GAPS - 1, "dve", "gates", PH - 1)
    return plan


def schedule():
    plan = front_plan()
    engines = ("pe", "act", "dve")
    ahead = [{e: [(0, s) for s in gap[e]] for e in engines} for gap in plan[:START]]
    ahead.append({"pe": [(0, s) for s in plan[START]["pe"] + plan[START + 2]["pe"]],
                  "act": [(0, ("pq_out", 2)), (0, ("ps_out", 2)), (0, ("pq_out", 3)), (0, ("ps_out", 3))],
                  "dve": [(0, ("place", 0)), (0, ("gates", 0))]})
    done = {("pq_out", 2), ("pq_out", 3), ("ps_out", 2), ("ps_out", 3), ("place", 0), ("gates", 0)}
    inside = [[{e: [] for e in engines} for _ in range(GAPS)] for _ in range(TILES)]
    for gap in range(START, GAPS):
        for e in ("act", "dve"):
            inside[0][gap - START][e] += [(0, s) for s in plan[gap][e] if s not in done]
    for t in range(TILES - 1):
        for gap in range(GAPS):
            for e in engines:
                inside[t][gap][e] += [(t + 1, s) for s in plan[gap][e]]
    return ahead, inside


START = 20
AHEAD, INSIDE = schedule()


def wide_order():
    names = ["kc", "vc", "ks", "kw", "q0", "q1", "q2", "q3", "vs", "vw", "gt", "hidk", "hidv", "h0", "c0", "b0",
             "kcc", "vcc"] + [f"{s}{c}" for c in range(1, CC) for s in "hcb"]
    for gap in AHEAD + [gap for tile in INSIDE for gap in tile]:
        for t, step in gap["pe"]:
            if step[0] == "cmp_scores":
                names += [("sc", t, 0), ("sc", t, 1)]
            elif step[0] == "cmp_values":
                names += [("oc", t)]
            elif step[0] in ("scores", "yc", "ya", "pq", "ps"):
                names += [(step[0], t, step[1])]
    return {name: n for n, name in enumerate(names)}


def turn_order():
    names = [("x", t, i) for t in range(TILES) for i in range(2)]
    for t in range(TILES):
        names += [("pc", t)] + [("p", t, n) for n in range(NBH)] + [("at", t), ("x2", t, 0), ("x2", t, 1)]
    return {name: n for n, name in enumerate(names)}


def layer(nc, A, out):
    WIDE, TURN = wide_order(), turn_order()
    with ExitStack() as ctx:
        def sb(name, shape, dt=F32):
            return ctx.enter_context(nc.sbuf_tensor(name, shape, dt))

        def sem(name):
            return ctx.enter_context(nc.semaphore(name))

        wide = ctx.enter_context(nc.psum_tensor("wide", [P, 2, 512], F32))
        turn = ctx.enter_context(nc.psum_tensor("turn", [P, 2, 512], F32))
        att_ps = ctx.enter_context(nc.psum_tensor("att_ps", [P, 2, 512], F32))
        acc = ctx.enter_context(nc.psum_tensor("acc", [P, 2, 512], F32))

        ring = sb("ring", [P, RING, 2 * D])
        stream = sb("stream", [P, SLOTS, D])
        w_out = sb("w_out_sb", [P, DC, D])
        subk = sb("subk", [P, HC, P])
        qT = sb("qT", [P, HPG, SEQ])
        kT = sb("kT", [P, 2, SEQ])
        vtok = sb("vtok", [P, TILES, 2, P])
        convT = sb("convT", [P, CC, SEQ])
        ln2 = sb("ln2_sb", [P, D])
        lnf = sb("lnf", [P, D])
        xh = sb("xh", [P, 2, D])
        xn2 = sb("xn2", [P, 2, D])
        ident = sb("ident", [P, P])
        causal = sb("causal", [P, P])
        cmask = sb("cmask", [P, TILES, NB])
        has_c = sb("has_c", [P, 1])
        iota16 = sb("iota16", [P, TOPK])
        iota16i = sb("iota16i", [P, TOPK], mybir.dt.int32)
        mean_col = sb("mean_col", [P, 1])
        ln1 = sb("ln1_sb", [P, DC])
        convw = sb("convw", [P, CC, 3])
        gnc = sb("gnc", [P, CC])
        gna = sb("gna", [P, CC])
        pos = sb("pos", [P, 2, LPAIRS])
        sig = sb("sig", [P, TILES, 3, HEADS])
        kcc = sb("kcc", [P, NB])
        vbd = sb("vbd", [P, GROUPS, HPG, HD])
        stat = sb("stat", [P, 8])
        newton = sb("newton", [P, 3, TILES])
        rstd_c = sb("rstd_c", [P, TILES])
        mean_x = sb("mean_x", [P, TILES])
        rstd_x = sb("rstd_x", [P, TILES])
        probs = sb("probs", [P, 2, 512])
        probsT = sb("probsT", [P, 2, 512])
        attn = sb("attn", [P, 512])
        atmp = sb("atmp", [P, 512])
        attT = sb("attT", [P, 512])
        xT2 = probs[:, :, :].rearrange("p a b -> p (a b)")
        pq = probsT
        pcs = sb("pcs", [P, GROUPS, HPG, NB])
        pcT = sb("pcT", [P, GROUPS, P])
        cmax = sb("cmax", [P, HEADS])
        csum = sb("csum", [P, HEADS])
        nmax = sb("nmax", [P, NBH])
        sums = sb("sums", [P, 2, HEADS])
        coef = sb("coef", [P, HEADS])
        keys_s = sb("keys_s", [P, 4, 4, P])
        cand = sb("cand", [P, TOPK, TOPK])
        onehot = atmp[:, :].rearrange("p (c k j) -> p c k j", c=2, k=TOPK)
        sv = sb("sv", [P, 2, TOPK])
        si = sb("si", [P, 2, TOPK], U32)
        sif = sb("sif", [P, 2, TOPK])
        best = sb("best", [P, TOPK])
        bi = sb("bi", [P, TOPK], U32)
        bhl = sb("bhl", [P, 2, TOPK], U32)
        bhlf = sb("bhlf", [P, 2, TOPK])
        ij = sb("ij", [P, 2, TOPK])
        bdiff = sb("bdiff", [P, TOPK])
        bexp = sb("bexp", [P, 2, TOPK])
        bsum = sb("bsum", [P, 2])
        brec = sb("brec", [P, 1])
        idx = sb("idx", [P, TILES, KTOT], U32)
        gate = sb("gate", [P, TILES * KTOT])
        ph = sb("ph", [P, 2, GRP])
        pt1 = sb("pt1", [P, GRP])
        pt2 = sb("pt2", [P, GRP])
        pt3 = sb("pt3", [P, GRP])
        pth = sb("pth", [P, 2, GRP])
        pa = sb("pa", [P, 2, GRP])
        diag = sb("diag", [P, GPE, P])

        flat = ring[:, :, :].rearrange("p a b -> p (a b)")
        xs = flat[:, 0:4096].rearrange("p (t d) -> p t d", t=TILES)
        sq_x = flat[:, 4096:7168].rearrange("p (a d) -> p a d", a=3)
        xnT = flat[:, 8192:12288].rearrange("p (c s) -> p c s", c=DC)
        kvc = flat[:, 12288:13312].rearrange("p (a s) -> p a s", a=2)
        kv2 = flat[:, 13312:15360].rearrange("p (a g s) -> p a g s", a=2, g=GROUPS)
        kvb = flat[:, 5120:7104].rearrange("p (a m n) -> p a m n", a=2, m=LPAIRS)
        ht = flat[:, 7168:7416].rearrange("p (a h n) -> p a h n", a=2, h=2)
        w2k = flat[:, 7424:7680].rearrange("p (h n) -> p h n", h=2)
        w2v = flat[:, 7680:7808].rearrange("p (h n) -> p h n", h=2)
        wg = flat[:, 7808:8000].rearrange("p (c n) -> p c n", c=DC)
        hx = flat[:, 15360:15608].rearrange("p (a h n) -> p a h n", a=2, h=2)
        hidk = flat[:, 15616:15744].rearrange("p (h g n) -> p h g n", h=2, g=GROUPS)
        hidv = flat[:, 15744:16256].rearrange("p (h g j n) -> p h g j n", h=2, g=GROUPS, j=HPG)
        zc = flat[:, 0:1040].rearrange("p (a s) -> p a s", a=2)
        chs = flat[:, 1040:2064].rearrange("p (a s) -> p a s", a=2)
        cacc = flat[:, 2064:3088].rearrange("p (a s) -> p a s", a=2)
        sqc = flat[:, 5120:6144].rearrange("p (a s) -> p a s", a=2)
        cout = flat[:, 6144:7168].rearrange("p (a s) -> p a s", a=2)

        params = sem("params")
        ln1_in = sem("ln1_in")
        x_in = [sem(f"x_in{t}") for t in range(TILES)]
        xh_in = [sem(f"xh_in{i}") for i in range(2)]
        w_out_in = sem("w_out_in")
        streamed = [sem(f"streamed{i}") for i in range(SLOTS)]
        stream_used = sem("stream_used")
        consts = sem("consts")
        wide_full = [sem(f"wide_full{i}") for i in range(2)]
        wide_free = [sem(f"wide_free{i}") for i in range(2)]
        turn_full = [sem(f"turn_full{i}") for i in range(2)]
        turn_free = [sem(f"turn_free{i}") for i in range(2)]
        vorder = sem("vorder")
        x_squared = sem("x_squared")
        x_squared2 = sem("x_squared2")
        rstd_ready = sem("rstd_ready")
        xs_ready = sem("xs_ready")
        xs_ready2 = sem("xs_ready2")
        kvb_ready = sem("kvb_ready")
        kv2_in = sem("kv2_in")
        hid_poly = sem("hid_poly")
        hid_tanh = sem("hid_tanh")
        hid_ready = sem("hid_ready")
        conv_ready = sem("conv_ready")
        ssq_done = sem("ssq_done")
        mean_done = sem("mean_done")
        cmp_shifted = sem("cmp_shifted")
        cmp_exp = sem("cmp_exp")
        max_ready = sem("max_ready")
        pv_done = sem("pv_done")
        att_free = sem("att_free")
        attn_ready = sem("attn_ready")
        keys_used = sem("keys_used")
        bdiff_ready = sem("bdiff_ready")
        bexp_ready = sem("bexp_ready")
        idx_ready = sem("idx_ready")
        xn2_ready = sem("xn2_ready")
        landed = [sem(f"landed{i}") for i in range(RING)]
        h_ready = sem("h_ready")
        gelu_step = sem("gelu_step")
        tanh_ready = sem("tanh_ready")
        diag_ready = sem("diag_ready")
        combined = sem("combined")
        vcombined = sem("vcombined")
        acc_read = sem("acc_read")
        out_ready = sem("out_ready")
        out_done = sem("out_done")

        N_PARAMS = 10

        def wait_full(eng, full, use):
            eng.wait_ge(full[use % 2], use // 2 + 1)

        def wait_read(eng, free, use):
            eng.wait_ge(free[use % 2], use // 2 + 1)

        def wait_free(eng, free, use):
            if use >= 2:
                eng.wait_ge(free[use % 2], use // 2)

        block = ctx.enter_context(nc.Block())

        @block.sync
        def _(sp):
            for t in range(TILES):
                sp.dma_start(xs[:, t, :], A["x"][0, t * P:(t + 1) * P, :]).then_inc(x_in[t], 16)
            sp.dma_start(ln1[:], A["ln1"]).then_inc(ln1_in, 16)

            def piece(n, src):
                if n >= SLOTS:
                    sp.wait_ge(stream_used, n - SLOTS + 1)
                sp.dma_start(stream[:, n % SLOTS, :], src).then_inc(streamed[n % SLOTS], 16)

            for n in range(SLOTS):
                piece(n, A["wpack"][n])
            for dst, name in ((pos[:], "pos"), (wg, "wg"), (w2k, "w2k"), (w2v, "w2v"), (convw[:], "convw"),
                              (gnc[:], "gnc"), (gna[:], "gna"), (subk[:], "subk")):
                sp.dma_start(dst, A[name]).then_inc(params, 16)
            sp.dma_start(ln2[:], A["ln2"].to_broadcast([P, D])).then_inc(params, 16)
            sp.dma_start(lnf[:], A["lnf"].to_broadcast([P, D])).then_inc(params, 16)
            for n in range(SLOTS, 9):
                piece(n, A["wpack"][n])
            wait_read(sp, wide_free, WIDE["kc"])
            wait_read(sp, wide_free, WIDE["vc"])
            for a in range(2):
                for g in range(GROUPS):
                    sp.dma_start(kv2[0:HD, a, g, :], kvc[g * HD:(g + 1) * HD, a, :]).then_inc(kv2_in, 16)
                    sp.dma_start(kv2[HD:P, a, g, 0:SEQ - 1], kvc[g * HD:(g + 1) * HD, a, 1:SEQ]).then_inc(kv2_in, 16)
            for n in range(9, N1):
                piece(n, A["wpack"][n])
            sp.dma_start(w_out[:], A["w_out"]).then_inc(w_out_in, 16)

            def store(t):
                sp.wait_ge(out_ready, t + 1)
                sp.dma_start(out[0, t * P:(t + 1) * P, :], xn2[:, t % 2, :]).then_inc(out_done, 16)

            for t in range(TILES):
                if t >= 2:
                    store(t - 2)
                sp.dma_start(xh[:, t % 2, :], A["x"][0, t * P:(t + 1) * P, :]).then_inc(xh_in[t % 2], 16)
                for i in range(HC):
                    piece(N1 + t * HC + i, A["wq"][i])
            for t in range(TILES - 2, TILES):
                store(t)
            sp.wait_ge(out_done, 16 * TILES)

        @block.gpsimd
        def _(pool):
            for z in (ident[:], causal[:], cmask[:], hidk, hidv, vbd[:]):
                nc.gpsimd.memset(z, 0.0).then_inc(consts, 1)
            nc.gpsimd.memset(has_c[:], 1.0).then_inc(consts, 1)
            nc.gpsimd.memset(mean_col[:], 1.0 / 512).then_inc(consts, 1)
            nc.gpsimd.iota(iota16i[:], pattern=[[1, TOPK]], base=0, channel_multiplier=0).then_inc(consts, 1)
            pool.wait_ge(consts, 9)
            nc.gpsimd.affine_select(out=ident[:], in_=ident[:], compare_op=ALU.not_equal, fill=1.0, base=0,
                                    pattern=[[-1, P]], channel_multiplier=1).then_inc(consts, 1)
            nc.gpsimd.affine_select(out=causal[:], in_=causal[:], compare_op=ALU.is_ge, fill=NEG, base=0,
                                    pattern=[[-1, P]], channel_multiplier=1).then_inc(consts, 1)
            nc.gpsimd.affine_select(out=cmask[:], in_=cmask[:], compare_op=ALU.is_ge, fill=NEG, base=-31,
                                    pattern=[[P, TILES], [-16, NB]], channel_multiplier=1).then_inc(consts, 1)
            nc.gpsimd.affine_select(out=has_c[:], in_=has_c[:], compare_op=ALU.is_ge, fill=0.0, base=-31,
                                    pattern=[[0, 1]], channel_multiplier=1).then_inc(consts, 1)
            nc.gpsimd.tensor_copy(iota16[:], iota16i[:]).then_inc(consts, 1)
            for t in range(TILES):
                for k in range(KTOT):
                    n = t * KTOT + k
                    if k % TOPK == 0:
                        pool.wait_ge(idx_ready, t * PH + k // TOPK + 1)
                    if n >= RING:
                        group, j = n // GRP - 2, n % GRP
                        if j < GPE:
                            pool.wait_ge(combined, GPE * group + j + 1)
                        else:
                            pool.wait_ge(vcombined, group + 1)
                    nc.gpsimd.indirect_dma_start(
                        out=ring[:, n % RING, :], out_offset=None, in_=A["uv"],
                        in_offset=bass.IndirectOffsetOnAxis(ap=idx[:, t, k:k + 1], axis=0),
                    ).then_inc(landed[n % RING], 16)

        CONSTS = 14

        @block.scalar
        def _(act):
            def evac(name, dst, scale=1.0):
                use = WIDE[name]
                wait_full(act, wide_full, use)
                nc.scalar.activation(dst, wide[:, use % 2, :], ACT.Copy, scale=scale).then_inc(wide_free[use % 2], 1)

            for t in (1, 3):
                act.wait_ge(x_in[t], 16)
                if t == 3:
                    act.wait_ge(x_squared2, 1)
                nc.scalar.activation(sq_x[:, 2, :], xs[:, t, :], ACT.Square, scale=D ** -0.5,
                                     accum_out=mean_x[:, t:t + 1]).then_inc(x_squared2, 1)
            act.wait_ge(rstd_ready, 1)
            for t in (1, 3):
                nc.scalar.activation(xs[:, t, :], xs[:, t, :], ACT.Copy, scale=rstd_x[:, t:t + 1]).then_inc(xs_ready2, 1)
            act.wait_ge(consts, CONSTS)
            for a, name in enumerate(("kc", "vc")):
                evac(name, kvc[:, a, :])
            for a, name in enumerate(("ks", "kw")):
                evac(name, kT[:, a, :])
            for j in range(HPG):
                evac(f"q{j}", qT[:, j, :], scale=HD ** -0.5)
            for b, name in enumerate(("vs", "vw")):
                wait_full(act, wide_full, WIDE[name])
                use = WIDE[name]
                nc.scalar.activation(vtok[:, :, b, :], wide[:, use % 2, :].rearrange("p (t c) -> p t c", t=TILES),
                                     ACT.Copy).then_inc(wide_free[use % 2], 1)
            use = WIDE["gt"]
            wait_full(act, wide_full, use)
            nc.scalar.activation(sig[:, :, :, :].rearrange("p t a h -> p (t a h)"), wide[:, use % 2, 0:96], ACT.Exp,
                                 scale=-1.0).then_inc(wide_free[use % 2], 1)

            def hidden_tanh(a):
                act.wait_ge(hid_poly, a + 1)
                nc.scalar.activation(ht[:, a, :, :], ht[:, a, :, :], ACT.Tanh, scale=GELU_C).then_inc(hid_tanh, 1)

            def conv_in(c):
                if c >= 2:
                    wait_read(act, wide_free, WIDE[f"c{c - 2}"])
                evac(f"h{c}", chs[:, c % 2, :])

            def conv_out(c):
                wait_read(act, wide_free, WIDE[f"b{c}"])
                if c >= 2:
                    act.wait_ge(ssq_done, c - 1)
                nc.scalar.activation(sqc[:, c % 2, :], cout[:, c % 2, :], ACT.Square).then_inc(conv_ready, 1)
                nc.scalar.activation(convT[:, c, :], cout[:, c % 2, :], ACT.Copy,
                                     scale=gnc[:, c:c + 1]).then_inc(conv_ready, 1)

            act.wait_ge(params, 16 * N_PARAMS)
            hidden_tanh(0)
            hidden_tanh(1)
            conv_in(0)
            use = WIDE["kcc"]
            wait_full(act, wide_full, use)
            nc.scalar.activation(kcc[0:HD, :], wide[0:HD, use % 2, 0:NB], ACT.Copy)
            nc.scalar.activation(kcc[HD:P, :], wide[HD:P, use % 2, NB:2 * NB], ACT.Copy).then_inc(wide_free[use % 2], 1)
            use = WIDE["vcc"]
            wait_full(act, wide_full, use)
            for j in range(HPG):
                rows = slice(j * NB, (j + 1) * NB)
                ins = nc.scalar.activation(vbd[rows, :, j, :],
                                           wide[rows, use % 2, 0:P].rearrange("p (g d) -> p g d", g=2), ACT.Copy)
            ins.then_inc(wide_free[use % 2], 1)
            conv_out(0)
            for c in range(1, CC):
                conv_in(c)
                conv_out(c)

            def probs_exp(t, n):
                keys = (t + 1) * P
                b, h = BRANCH_HEADS[n]
                use = WIDE[("scores", t, n)]
                act.wait_ge(max_ready, t * NBH + n + 1)
                if n >= 2:
                    wait_full(act, turn_full, TURN[("p", t, n - 2)])
                elif t >= 1:
                    wait_full(act, wide_full, WIDE[("pq", t - 1, 3)])
                nc.scalar.activation(probs[:, n % 2, 0:keys], wide[:, use % 2, 0:keys], ACT.Exp,
                                     bias=nmax[:, n:n + 1], accum_out=sums[:, b, h:h + 1]).then_inc(wide_free[use % 2], 1)

            def probs_turn(t, n):
                keys = (t + 1) * P
                use = TURN[("p", t, n)]
                wait_full(act, turn_full, use)
                if n >= 2:
                    act.wait_ge(pv_done, t * NBH + n - 1)
                nc.scalar.activation(probsT[:, n % 2, 0:keys], turn[:, use % 2, 0:keys],
                                     ACT.Copy).then_inc(turn_free[use % 2], 1)

            def step(t, name, i=0):
                if name == "cmp_exp":
                    act.wait_ge(cmp_shifted, t + 1)
                    nc.scalar.activation(pcs[:], pcs[:], ACT.Exp).then_inc(cmp_exp, 1)
                elif name == "cmp_turned":
                    use = TURN[("pc", t)]
                    wait_full(act, turn_full, use)
                    nc.scalar.activation(pcT[:, :, :].rearrange("p g q -> p (g q)"), turn[:, use % 2, 0:2 * P],
                                         ACT.Copy).then_inc(turn_free[use % 2], 1)
                elif name == "exp":
                    probs_exp(t, i)
                elif name == "turned":
                    probs_turn(t, i)
                elif name == "x2_turned":
                    for k in range(2):
                        use = TURN[("x2", t, k)]
                        wait_full(act, turn_full, use)
                        nc.scalar.activation(xT2[:, k * 512:(k + 1) * 512], turn[:, use % 2, :],
                                             ACT.Copy).then_inc(turn_free[use % 2], 1)
                elif name == "pq_out":
                    evac(("pq", t, i), pq[:, i % 2, :])
                elif name == "ps_out":
                    if t >= 1:
                        act.wait_ge(keys_used, PH * (t - 1) + 2 * (i + 1))
                    evac(("ps", t, i), keys_s[:, i, :, :].rearrange("p a n -> p (a n)"))
                elif name == "best_exp":
                    act.wait_ge(bdiff_ready, t * PH + i + 1)
                    nc.scalar.activation(bexp[:, i % 2, :], bdiff[:], ACT.Exp,
                                         accum_out=bsum[:, i % 2:i % 2 + 1]).then_inc(bexp_ready, 1)

            def group(i, q, first=False):
                act.wait_ge(gelu_step, 10 * i + 5 * q + 3)
                nc.scalar.activation(pth[:, q, :], pt3[:], ACT.Tanh, scale=GELU_C).then_inc(tanh_ready, 1)
                act.wait_ge(gelu_step, 10 * i + 5 * q + 5)
                for j in range(GPE):
                    if not first:
                        act.wait_ge(combined, 2 * GPE * i + GPE * q + j + 1 - GPE)
                    nc.scalar.activation(diag[:, j, :], ident[:], ACT.Copy,
                                         scale=pa[:, q, j:j + 1]).then_inc(diag_ready, 1)

            run_plan("act", step, group, nc.scalar.Fori)

        @block.tensor
        def _(pe):
            held = [False]

            def piece(n):
                pe.wait_ge(streamed[n % SLOTS], 16 * (n // SLOTS + 1))
                return stream[:, n % SLOTS, :]

            def let_go(ins):
                if held[0]:
                    ins.then_inc(stream_used, 1)
                held[0] = False

            def transposes(name, srcs, rows=P):
                use = TURN[name]
                wait_free(pe, turn_free, use)
                for i, s in enumerate(srcs):
                    ins = nc.tensor.transpose(turn[:, use % 2, i * P:(i + 1) * P], s, ident[:])
                ins.then_inc(turn_full[use % 2], 1)

            pe.wait_ge(consts, CONSTS)
            for t in range(TILES):
                pe.wait_ge(xs_ready if t % 2 == 0 else xs_ready2, t // 2 + 1)
                for i in range(2):
                    transposes(("x", t, i), [xs[:, t, (4 * i + c) * P:(4 * i + c + 1) * P] for c in range(4)])
            for i in range(2):
                pe.wait_ge(turn_free[i], TILES)
            def channels(name):
                w = piece(STREAM1.index(name)).rearrange("p (c n) -> p c n", c=DC)
                use = WIDE[name]
                wait_free(pe, wide_free, use)
                for c in range(DC):
                    ins = nc.tensor.matmul(wide[:, use % 2, :], w[:, c, :], xnT[:, c, :], start=(c == 0),
                                           stop=(c == DC - 1))
                    if c == 0:
                        let_go(ins)
                ins.then_inc(wide_full[use % 2], 1)
                held[0] = True

            def tokens(name, w, cols):
                use = WIDE[name]
                wait_free(pe, wide_free, use)
                for t in range(TILES):
                    for c in range(DC):
                        ins = nc.tensor.matmul(wide[:, use % 2, t * cols:(t + 1) * cols],
                                               xnT[:, c, t * P:(t + 1) * P], w[:, c, :],
                                               start=(c == 0), stop=(c == DC - 1))
                        let_go(ins)
                ins.then_inc(wide_full[use % 2], 1)

            for name in ("kc", "vc", "ks", "kw", "q0", "q1", "q2", "q3"):
                channels(name)
            for name in ("vs", "vw"):
                tokens(name, piece(STREAM1.index(name)).rearrange("p (c n) -> p c n", c=DC), P)
                held[0] = True
            pe.wait_ge(params, 16 * N_PARAMS)
            tokens("gt", wg, 24)

            def hidden(a):
                name = "kv"[a]
                use = WIDE[f"hid{name}"]
                wait_free(pe, wide_free, use)
                pe.wait_ge(kvb_ready, a + 1)
                o = wide[:, use % 2, :]
                for m in range(LPAIRS):
                    if m % 4 == 0:
                        w = piece(STREAM1.index(f"w1{name}{m // 4}")).rearrange("p (m n) -> p m n", m=4)
                    for hh in range(2):
                        lhs = w[:, m % 4, hh * P:(hh + 1) * P]
                        ins = nc.tensor.matmul(o[:, hh * 62:hh * 62 + 62], lhs, kvb[:, a, m, :],
                                               start=(m == 0 and hh == 0), stop=(m == LPAIRS - 1),
                                               skip_group_check=True)
                        let_go(ins)
                    held[0] = m % 4 == 3
                ins.then_inc(wide_full[use % 2], 1)

            hidden(0)
            hidden(1)

            def conv(c):
                for s in "hcb":
                    channels(f"{s}{c}")

            def conv_squares(c):
                pe.wait_ge(conv_ready, 2 * c + 1)
                for t in range(TILES):
                    ins = nc.tensor.matmul(att_ps[:, 0, t:t + 1], sqc[:, c % 2, t * P:(t + 1) * P], mean_col[:],
                                           start=(c == 0 and t == 0), stop=(c == CC - 1), skip_group_check=True)
                    let_go(ins)
                ins.then_inc(ssq_done, 1)

            conv(0)
            pe.wait_ge(hid_ready, 2)
            use = WIDE["kcc"]
            wait_free(pe, wide_free, use)
            for hh in range(2):
                ins = nc.tensor.matmul(wide[:, use % 2, 0:2 * NB], w2k[:, hh, :],
                                       hidk[:, hh, :, :].rearrange("p g n -> p (g n)"), start=(hh == 0), stop=(hh == 1))
            ins.then_inc(wide_full[use % 2], 1)
            use = WIDE["vcc"]
            wait_free(pe, wide_free, use)
            for g in range(GROUPS):
                for hh in range(2):
                    ins = nc.tensor.matmul(wide[:, use % 2, g * HD:(g + 1) * HD],
                                           hidv[:, hh, g, :, :].rearrange("p j n -> p (j n)"), w2v[:, hh, :],
                                           start=(hh == 0), stop=(hh == 1))
            ins.then_inc(wide_full[use % 2], 1)
            for c in range(1, CC):
                conv(c)
                conv_squares(c - 1)
            conv_squares(CC - 1)

            def scores(t, n):
                b, h = BRANCH_HEADS[n]
                g, j = h // HPG, h % HPG
                rows = slice(g * HD, (g + 1) * HD)
                use = WIDE[("scores", t, n)]
                wait_free(pe, wide_free, use)
                nc.tensor.matmul(wide[:, use % 2, 0:(t + 1) * P], qT[rows, j, t * P:(t + 1) * P],
                                 kT[rows, b, 0:(t + 1) * P], start=True, stop=True).then_inc(wide_full[use % 2], 1)

            def values(t, n):
                b, h = BRANCH_HEADS[n]
                use = TURN[("p", t, n)]
                wait_read(pe, turn_free, use)
                if n % HEADS == 0:
                    if t >= 1:
                        pe.wait_ge(att_free, 2 * (t - 1) + b + 1)
                    elif b == 0:
                        pe.wait_ge(mean_done, 1)
                for kb in range(t + 1):
                    ins = nc.tensor.matmul(att_ps[:, b, h * HD:(h + 1) * HD], probsT[:, n % 2, kb * P:(kb + 1) * P],
                                           vtok[:, kb, b, (h // HPG) * HD:(h // HPG + 1) * HD],
                                           start=(kb == 0), stop=(kb == t))
                ins.then_inc(pv_done, 1)

            def step(t, name, i=0):
                if name == "cmp_scores":
                    if t == 0:
                        wait_read(pe, wide_free, WIDE["kcc"])
                    for g in range(GROUPS):
                        use = WIDE[("sc", t, g)]
                        wait_free(pe, wide_free, use)
                        rows = slice(g * HD, (g + 1) * HD)
                        for j in range(HPG):
                            ins = nc.tensor.matmul(wide[:, use % 2, j * NB:(j + 1) * NB], qT[rows, j, t * P:(t + 1) * P],
                                                   kcc[rows, :], start=True, stop=True)
                        ins.then_inc(wide_full[use % 2], 1)
                elif name == "cmp_turn":
                    pe.wait_ge(cmp_exp, t + 1)
                    transposes(("pc", t), [pcs[:, g, :, :].rearrange("p j n -> p (j n)") for g in range(GROUPS)])
                elif name == "cmp_values":
                    wait_read(pe, turn_free, TURN[("pc", t)])
                    if t == 0:
                        wait_read(pe, wide_free, WIDE["vcc"])
                    use = WIDE[("oc", t)]
                    wait_free(pe, wide_free, use)
                    for g in range(GROUPS):
                        ins = nc.tensor.matmul(wide[:, use % 2, g * 256:(g + 1) * 256], pcT[:, g, :],
                                               vbd[:, g, :, :].rearrange("p j d -> p (j d)"), start=True, stop=True)
                    ins.then_inc(wide_full[use % 2], 1)
                elif name == "scores":
                    scores(t, i)
                elif name == "turn":
                    wait_read(pe, wide_free, WIDE[("scores", t, i)])
                    transposes(("p", t, i), [probs[:, i % 2, kb * P:(kb + 1) * P] for kb in range(t + 1)])
                elif name == "values":
                    values(t, i)
                elif name == "att_turn":
                    pe.wait_ge(attn_ready, t + 1)
                    transposes(("at", t), [attn[:, c * P:(c + 1) * P] for c in range(CC)])
                elif name in ("yc", "ya"):
                    use = WIDE[(name, t, i)]
                    wait_free(pe, wide_free, use)
                    if t == 0 and name == "yc":
                        pe.wait_ge(w_out_in, 16)
                        pe.wait_ge(conv_ready, 2 * CC)
                    if name == "ya":
                        wait_read(pe, turn_free, TURN[("at", t)])
                    for c in range(CC):
                        lhs = convT[:, c, t * P:(t + 1) * P] if name == "yc" else attT[:, c * P:(c + 1) * P]
                        ins = nc.tensor.matmul(wide[:, use % 2, :], lhs,
                                               w_out[:, c + CC * (name == "ya"), i * 512:(i + 1) * 512],
                                               start=(c == 0), stop=(c == CC - 1))
                    ins.then_inc(wide_full[use % 2], 1)
                elif name == "x2_turn":
                    pe.wait_ge(xn2_ready, t + 1)
                    for k in range(2):
                        transposes(("x2", t, k), [xn2[:, t % 2, (4 * k + c) * P:(4 * k + c + 1) * P] for c in range(4)])
                elif name == "pq":
                    if i == 0:
                        for k in range(2):
                            wait_read(pe, turn_free, TURN[("x2", t, k)])
                    use = WIDE[("pq", t, i)]
                    wait_free(pe, wide_free, use)
                    for a in range(4):
                        w = piece(N1 + t * HC + 4 * i + a).rearrange("p (c n) -> p c n", c=DC)
                        for c in range(DC):
                            ins = nc.tensor.matmul(wide[:, use % 2, a * P:(a + 1) * P], w[:, c, :],
                                                   xT2[:, c * P:(c + 1) * P], start=(c == 0), stop=(c == DC - 1))
                            let_go(ins)
                        held[0] = True
                    ins.then_inc(wide_full[use % 2], 1)
                elif name == "ps":
                    wait_read(pe, wide_free, WIDE[("pq", t, i)])
                    use = WIDE[("ps", t, i)]
                    wait_free(pe, wide_free, use)
                    for a in range(4):
                        ins = nc.tensor.matmul(wide[:, use % 2, a * P:(a + 1) * P], pq[:, i % 2, a * P:(a + 1) * P],
                                               subk[:, 4 * i + a, :], start=True, stop=True)
                        let_go(ins)
                    ins.then_inc(wide_full[use % 2], 1)

            def group(i, q, first=False, start=False, stop=False):
                for j in range(GPE):
                    pe.wait_ge(diag_ready, 2 * GPE * i + GPE * q + j + 1)
                    for half in range(2):
                        ins = nc.tensor.matmul(acc[:, half, :], diag[:, j, :],
                                               ring[:, q * GRP + j, D + half * 512:D + (half + 1) * 512],
                                               start=start and j == 0, stop=stop and j == GPE - 1,
                                               skip_group_check=True)
                    ins.then_inc(combined, 1)

            def edge(i, q):
                start, stop = (i % ITERS, q) == (0, 0), (i % ITERS, q) == (ITERS - 1, 1)
                if start and i:
                    pe.wait_ge(acc_read, 2 * (i // ITERS))
                group(i, q, start=start, stop=stop)

            run_plan("pe", step, group, nc.tensor.Fori, edge)

        @block.vector
        def _(dve):
            v = nc.vector
            count = [0]

            def then(ins):
                count[0] += 1
                ins.then_inc(vorder, 1)
                dve.wait_ge(vorder, count[0])

            def bcast(ap, n):
                return ap.unsqueeze(2).to_broadcast([ap.shape[0], ap.shape[1], n])

            def rstd(dst, mean, last=None):
                n = dst.shape[1]
                x, y, e = (newton[:, k, 0:n] for k in range(3))
                then(v.tensor_scalar(x, mean, EPS, None, ALU.add))
                then(v.tensor_scalar(y.bitcast(U32), x.bitcast(U32), -0.5, float(0x5F3759DF), ALU.mult, ALU.add))
                for step in range(3):
                    then(v.tensor_tensor(e, y, y, ALU.mult))
                    then(v.tensor_tensor(e, e, x, ALU.mult))
                    then(v.tensor_scalar(e, e, -0.5, 1.5, ALU.mult, ALU.add))
                    ins = v.tensor_tensor(dst if step == 2 else y, y, e, ALU.mult)
                    if step == 2 and last is not None:
                        ins.then_inc(last, 1)
                    else:
                        then(ins)

            dve.wait_ge(consts, CONSTS)
            for t in (0, 2):
                dve.wait_ge(x_in[t], 16)
                v.tensor_tensor_reduce(sq_x[:, t // 2, :], xs[:, t, :], xs[:, t, :], 1.0 / D, 0.0, ALU.mult, ALU.add,
                                       mean_x[:, t:t + 1]).then_inc(x_squared, 1)
            dve.wait_ge(x_squared, 2)
            dve.wait_ge(x_squared2, 2)
            rstd(rstd_x[:], mean_x[:], rstd_ready)
            dve.wait_ge(rstd_ready, 1)
            for t in (0, 2):
                v.tensor_scalar(xs[:, t, :], xs[:, t, :], rstd_x[:, t:t + 1], None, ALU.mult).then_inc(xs_ready, 1)
            dve.wait_ge(ln1_in, 16)
            for t in range(TILES):
                for i in range(2):
                    use = TURN[("x", t, i)]
                    wait_full(dve, turn_full, use)
                    v.tensor_tensor(xnT[:, 4 * i:4 * i + 4, t * P:(t + 1) * P],
                                    turn[:, use % 2, :].rearrange("p (c q) -> p c q", c=4),
                                    bcast(ln1[:, 4 * i:4 * i + 4], P), ALU.mult).then_inc(turn_free[use % 2], 1)
            then(v.memset(zc[:, :, 0:2], 0.0))

            dve.wait_ge(params, 16 * N_PARAMS)
            dve.wait_ge(kv2_in, 16 * 8)
            for a in range(2):
                for g in range(GROUPS):
                    src = kv2[:, a, g, 0:SEQ]
                    for half in range(2):
                        n0 = half * 16
                        pairs = src[:, n0:n0 + 16 * NCMP].rearrange("p (n m r) -> p m n r", n=NCMP, m=8)[:, :, :, 0]
                        ins = v.tensor_tensor(kvb[:, a, 8 * half:8 * half + 8, g * NCMP:(g + 1) * NCMP], pairs,
                                              bcast(pos[:, a, 8 * half:8 * half + 8], NCMP), ALU.add)
                ins.then_inc(kvb_ready, 1)
            use = WIDE["gt"]
            wait_read(dve, wide_free, use)
            sg = sig[:, :, :, :].rearrange("p t a h -> p (t a h)")
            then(v.tensor_scalar(sg, sg, 1.0, None, ALU.add))
            then(v.reciprocal(sg, sg))

            def hidden(a):
                use = WIDE["hid" + "kv"[a]]
                wait_full(dve, wide_full, use)
                o = wide[:, use % 2, 0:124]
                hxa, hta = (z[:, a, :, :].rearrange("p h n -> p (h n)") for z in (hx, ht))
                then(v.tensor_copy(hxa, o))
                v.tensor_tensor(hta, hxa, hxa, ALU.mult).then_inc(wide_free[use % 2], 1)
                wait_read(dve, wide_free, use)
                then(v.tensor_scalar(hta, hta, 0.044715, 1.0, ALU.mult, ALU.add))
                v.tensor_tensor(hta, hta, hxa, ALU.mult).then_inc(hid_poly, 1)

            def hidden_out(a):
                dve.wait_ge(hid_tanh, a + 1)
                hxa, hta = (z[:, a, :, :].rearrange("p h n -> p (h n)") for z in (hx, ht))
                then(v.scalar_tensor_tensor(hta, hta, 1.0, hxa, ALU.add, ALU.mult))
                for hh in range(2):
                    src = ht[:, a, hh, :].rearrange("p (g n) -> p g n", g=2)
                    if a == 0:
                        ins = v.tensor_scalar(hidk[:, hh, :, 0:NCMP], src, 0.5, None, ALU.mult)
                    else:
                        for j in range(HPG):
                            ins = v.tensor_scalar(hidv[:, hh, :, j, 0:NCMP], src, 0.5, None, ALU.mult)
                ins.then_inc(hid_ready, 1)

            hidden(0)
            hidden(1)
            hidden_out(0)
            hidden_out(1)

            for c in range(CC):
                b = c % 2
                use = WIDE[f"h{c}"]
                wait_read(dve, wide_free, use)
                use = WIDE[f"c{c}"]
                wait_full(dve, wide_full, use)
                v.tensor_tensor(zc[:, b, 2:514], chs[:, b, :], wide[:, use % 2, :],
                                ALU.mult).then_inc(wide_free[use % 2], 1)
                wait_read(dve, wide_free, use)
                then(v.tensor_scalar(cacc[:, b, :], zc[:, b, 0:512], convw[:, c, 0:1], None, ALU.mult))
                for k in (1, 2):
                    then(v.scalar_tensor_tensor(cacc[:, b, :], zc[:, b, k:k + 512], convw[:, c, k:k + 1],
                                                cacc[:, b, :], ALU.mult, ALU.add))
                use = WIDE[f"b{c}"]
                wait_full(dve, wide_full, use)
                if c >= 2:
                    dve.wait_ge(conv_ready, 2 * (c - 1))
                v.tensor_tensor(cout[:, b, :], cacc[:, b, :], wide[:, use % 2, :],
                                ALU.mult).then_inc(wide_free[use % 2], 1)
            dve.wait_ge(ssq_done, CC)
            then(v.tensor_copy(rstd_c[:], att_ps[:, 0, 0:TILES]))
            rstd(rstd_c[:], rstd_c[:], mean_done)

            def branch_out(t, b):
                dve.wait_ge(pv_done, t * NBH + HEADS * (b + 1))
                then(v.reciprocal(coef[:], sums[:, b, :]))
                then(v.tensor_tensor(coef[:], coef[:], sig[:, t, 1 + b, :], ALU.mult))
                then(v.tensor_tensor(atmp[:, :].rearrange("p (h d) -> p h d", h=HEADS),
                                     att_ps[:, b, :].rearrange("p (h d) -> p h d", h=HEADS), bcast(coef[:], HD),
                                     ALU.mult))
                v.tensor_tensor(attn[:], attn[:], atmp[:], ALU.add).then_inc(att_free, 1)
                dve.wait_ge(att_free, 2 * t + b + 1)

            def row_max(t, n):
                use = WIDE[("scores", t, n)]
                wait_full(dve, wide_full, use)
                own = wide[:, use % 2, t * P:(t + 1) * P]
                then(v.tensor_tensor(own, own, causal[:], ALU.add))
                if n == 0 and t >= 1:
                    wait_read(dve, wide_free, WIDE[("scores", t - 1, NBH - 1)])
                v.tensor_reduce(nmax[:, n:n + 1], wide[:, use % 2, 0:(t + 1) * P], AX_X, ALU.max,
                                negate=True).then_inc(max_ready, 1)

            def top16(src, vals, inds):
                then(v.max(vals[:, 0:8], src))
                then(v.max_index(inds[:, 0:8], vals[:, 0:8], src))
                then(v.match_replace(src, vals[:, 0:8], src, -3.0e38))
                then(v.max(vals[:, 8:16], src))
                then(v.max_index(inds[:, 8:16], vals[:, 8:16], src))

            def keys(t, h):
                wait_read(dve, wide_free, WIDE[("ps", t, h // 2)])
                for c in range(2):
                    top16(keys_s[:, h // 2, 2 * (h % 2) + c, :], sv[:, c, :], si[:, c, :])

            def candidates(t, h):
                v.tensor_tensor(cand[:], bcast(sv[:, 0, :], TOPK), sv[:, 1:2, :].to_broadcast([P, TOPK, TOPK]),
                                ALU.add).then_inc(keys_used, 1)
                dve.wait_ge(keys_used, t * PH + h + 1)
                top16(cand[:, :, :].rearrange("p a b -> p (a b)"), best, bi)
                m = t * PH + h
                if m >= 1:
                    dve.wait_ge(bexp_ready, m)
                v.tensor_scalar(bdiff[:], best[:], best[:, 0:1], None, ALU.subtract).then_inc(bdiff_ready, 1)

            def place(t, h):
                then(v.tensor_scalar(bhl[:, 0, :], bi[:], 4, None, ALU.logical_shift_right))
                then(v.tensor_scalar(bhl[:, 1, :], bi[:], 15, None, ALU.bitwise_and))
                then(v.tensor_copy(bhlf[:], bhl[:]))
                then(v.tensor_copy(sif[:], si[:]))
                oh = onehot.rearrange("p c k j -> p (c k) j")
                then(v.tensor_tensor(oh, bcast(bhlf[:, :, :].rearrange("p c k -> p (c k)"), TOPK),
                                     iota16[:].unsqueeze(1).to_broadcast([P, 2 * TOPK, TOPK]), ALU.is_equal))
                then(v.tensor_tensor(onehot, onehot, sif[:].unsqueeze(2).to_broadcast([P, 2, TOPK, TOPK]),
                                     ALU.mult))
                then(v.tensor_reduce(ij[:, :, :].rearrange("p c k -> p (c k)"), oh, AX_X, ALU.add))
                v.scalar_tensor_tensor(idx[:, t, h * TOPK:(h + 1) * TOPK], ij[:, 0, :], float(P), ij[:, 1, :],
                                       ALU.mult, ALU.add).then_inc(idx_ready, 1)

            def gates(t, h):
                m = t * PH + h
                dve.wait_ge(bexp_ready, m + 1)
                then(v.reciprocal(brec[:], bsum[:, h % 2:h % 2 + 1]))
                then(v.tensor_scalar(gate[:, m * TOPK:(m + 1) * TOPK], bexp[:, h % 2, :], brec[:], 0.5, ALU.mult,
                                     ALU.mult))

            def step(t, name, i=0):
                xhh = xh[:, t % 2, i * 512:(i + 1) * 512] if i < 2 else None
                if name == "cmp_shift":
                    for g in range(GROUPS):
                        use = WIDE[("sc", t, g)]
                        wait_full(dve, wide_full, use)
                        v.tensor_tensor(pcs[:, g, :, :], wide[:, use % 2, 0:P].rearrange("p (j n) -> p j n", j=HPG),
                                        cmask[:, t:t + 1, :].to_broadcast([P, HPG, NB]),
                                        ALU.add).then_inc(wide_free[use % 2], 1)
                        wait_read(dve, wide_free, use)
                    heads = pcs[:, :, :, :].rearrange("p g j n -> p (g j) n")
                    then(v.tensor_reduce(cmax[:], heads, AX_X, ALU.max))
                    v.tensor_tensor(heads, heads, bcast(cmax[:], NB), ALU.subtract).then_inc(cmp_shifted, 1)
                elif name == "cmp_coef":
                    dve.wait_ge(cmp_exp, t + 1)
                    then(v.tensor_reduce(csum[:], pcs[:, :, :, :].rearrange("p g j n -> p (g j) n"), AX_X, ALU.add))
                    then(v.reciprocal(coef[:], csum[:]))
                    then(v.tensor_tensor(coef[:], coef[:], sig[:, t, 0, :], ALU.mult))
                    if t == 0:
                        then(v.tensor_scalar(coef[:], coef[:], has_c[:], None, ALU.mult))
                elif name == "cmp_out":
                    use = WIDE[("oc", t)]
                    wait_full(dve, wide_full, use)
                    v.tensor_tensor(attn[:, :].rearrange("p (h d) -> p h d", h=HEADS),
                                    wide[:, use % 2, :].rearrange("p (h d) -> p h d", h=HEADS), bcast(coef[:], HD),
                                    ALU.mult).then_inc(wide_free[use % 2], 1)
                    wait_read(dve, wide_free, use)
                elif name == "max":
                    row_max(t, i)
                elif name == "branch":
                    branch_out(t, i)
                elif name == "att_norm":
                    then(v.tensor_tensor_reduce(atmp[:], attn[:], attn[:], 1.0 / 512, 0.0, ALU.mult, ALU.add,
                                                stat[:, 0:1]))
                    rstd(stat[:, 1:2], stat[:, 0:1])
                    v.tensor_scalar(attn[:], attn[:], stat[:, 1:2], None, ALU.mult).then_inc(attn_ready, 1)
                elif name == "att_turned":
                    use = TURN[("at", t)]
                    wait_full(dve, turn_full, use)
                    v.tensor_tensor(attT[:, :].rearrange("p (c q) -> p c q", c=CC),
                                    turn[:, use % 2, :].rearrange("p (c q) -> p c q", c=CC), bcast(gna[:], P),
                                    ALU.mult).then_inc(turn_free[use % 2], 1)
                elif name == "add_yc":
                    if i == 0:
                        dve.wait_ge(xh_in[t % 2], 16 * (t // 2 + 1))
                    use = WIDE[("yc", t, i)]
                    wait_full(dve, wide_full, use)
                    v.scalar_tensor_tensor(xhh, wide[:, use % 2, :], rstd_c[:, t:t + 1], xhh, ALU.mult,
                                           ALU.add).then_inc(wide_free[use % 2], 1)
                elif name == "norm2":
                    for half in range(2):
                        cols = slice(half * 512, (half + 1) * 512)
                        use = WIDE[("ya", t, half)]
                        wait_full(dve, wide_full, use)
                        wait_read(dve, wide_free, WIDE[("yc", t, half)])
                        v.tensor_tensor(xh[:, t % 2, cols], xh[:, t % 2, cols], wide[:, use % 2, :],
                                        ALU.add).then_inc(wide_free[use % 2], 1)
                        wait_read(dve, wide_free, use)
                    h1 = xh[:, t % 2, :]
                    if t >= 2:
                        dve.wait_ge(out_done, 16 * (t - 1))
                    then(v.tensor_tensor_reduce(xn2[:, t % 2, :], h1, h1, 1.0 / D, 0.0, ALU.mult, ALU.add, stat[:, 0:1]))
                    rstd(stat[:, 1:2], stat[:, 0:1])
                    v.scalar_tensor_tensor(xn2[:, t % 2, :], h1, stat[:, 1:2], ln2[:], ALU.mult,
                                           ALU.mult).then_inc(xn2_ready, 1)
                    dve.wait_ge(xn2_ready, t + 1)
                elif name == "keys":
                    keys(t, i)
                elif name == "cand":
                    candidates(t, i)
                elif name == "place":
                    place(t, i)
                elif name == "gates":
                    gates(t, i)

            def group(i, q, first=False, t=None):
                xt = xn2[:, t % 2, :]
                for j in range(GRP):
                    s = q * GRP + j
                    dve.wait_ge(landed[s], 16 * i + 16)
                    v.tensor_tensor_reduce(ring[:, s, 0:D], ring[:, s, 0:D], xt, 1.0, 0.0, ALU.mult, ALU.add,
                                           ph[:, q, j:j + 1]).then_inc(h_ready, 1)
                dve.wait_ge(h_ready, 8 * i + 4 * q + 4)
                v.tensor_tensor(pt1[:], ph[:, q, :], ph[:, q, :], ALU.mult).then_inc(gelu_step, 1)
                dve.wait_ge(gelu_step, 10 * i + 5 * q + 1)
                v.tensor_scalar(pt2[:], pt1[:], 0.044715, 1.0, ALU.mult, ALU.add).then_inc(gelu_step, 1)
                dve.wait_ge(gelu_step, 10 * i + 5 * q + 2)
                v.tensor_tensor(pt3[:], pt2[:], ph[:, q, :], ALU.mult).then_inc(gelu_step, 1)
                dve.wait_ge(tanh_ready, 2 * i + q + 1)
                v.scalar_tensor_tensor(pt2[:], pth[:, q, :], 1.0, ph[:, q, :], ALU.add, ALU.mult).then_inc(gelu_step, 1)
                dve.wait_ge(gelu_step, 10 * i + 5 * q + 4)
                v.tensor_tensor(pa[:, q, :], pt2[:], gate[:, bass.ds(i * RING + q * GRP, GRP)],
                                ALU.mult).then_inc(gelu_step, 1)
                dve.wait_ge(gelu_step, 10 * i + 5 * q + 5)
                if not first:
                    dve.wait_ge(vcombined, 2 * i + q)
                v.scalar_tensor_tensor(xh[:, t % 2, :], ring[:, q * GRP + GPE, D:2 * D], pa[:, q, GPE:GPE + 1],
                                       xh[:, t % 2, :], ALU.mult, ALU.add).then_inc(vcombined, 1)

            def finish(t):
                h1 = xh[:, t % 2, :]
                dve.wait_ge(combined, (t + 1) * 2 * ITERS * GPE)
                dve.wait_ge(vcombined, (t + 1) * 2 * ITERS)
                for half in range(2):
                    cols = slice(half * 512, (half + 1) * 512)
                    v.tensor_tensor(xh[:, t % 2, cols], xh[:, t % 2, cols], acc[:, half, :],
                                    ALU.add).then_inc(acc_read, 1)
                dve.wait_ge(acc_read, 2 * (t + 1))
                then(v.tensor_tensor_reduce(xn2[:, t % 2, :], h1, h1, 1.0 / D, 0.0, ALU.mult, ALU.add, stat[:, 2:3]))
                rstd(stat[:, 2:3], stat[:, 2:3])
                v.scalar_tensor_tensor(xn2[:, t % 2, :], h1, stat[:, 2:3], lnf[:], ALU.mult,
                                       ALU.mult).then_inc(out_ready, 1)

            run_plan("dve", step, group, nc.vector.Fori, finish=finish)


def run_plan(engine, step, group, fori, edge=None, finish=None):
    def one(t, i, q):
        if edge is not None and (i % ITERS, q) in ((0, 0), (ITERS - 1, 1)):
            edge(i, q)
        elif finish is not None:
            group(i, q, first=(i + q == 0), t=t)
        else:
            group(i, q, first=(i + q == 0))

    for gap in AHEAD:
        for tile, s in gap[engine]:
            step(tile, *s)
    for t in range(TILES):
        steps = {g: INSIDE[t][g][engine] for g in range(GAPS)}
        n = 0
        while n < 2 * ITERS:
            end = n
            while end < 2 * ITERS and not (end > n and steps.get(end - 1)) and not (edge and end == 2 * ITERS - 1):
                end += 1
            iters = (end - n) // 2
            if n % 2 == 0 and iters >= 2 and n > 0:
                with fori(t * ITERS + n // 2, t * ITERS + n // 2 + iters) as i:
                    for q in range(2):
                        group(i, q, **({"t": t} if finish is not None else {}))
                n += 2 * iters
            else:
                one(t, t * ITERS + n // 2, n % 2)
                n += 1
            for tile, s in steps.get(n - 1, []):
                step(tile, *s)
        if finish is not None:
            finish(t)


def kernel(x, ln1, w_in, conv_w, cmp_pos_k, cmp_pos_v, cmp_k_w1, cmp_k_w2, cmp_v_w1, cmp_v_w2,
           gn_conv, gn_attn, w_out, ln2, peer_wq, peer_subkeys, peer_u, peer_v, ln_f):
    import concourse.bacc as bacc
    from concourse.bass_utils import run_bass_kernel_spmd

    col = {}
    at = 0
    for name, n in (("h", 512), ("b", 512), ("c", 512), ("q", 512), ("kc", 128), ("vc", 128), ("ks", 128), ("vs", 128),
                    ("kw", 128), ("vw", 128), ("g", 24)):
        col[name] = w_in[0][:, at:at + n]
        at += n

    def rows(w):
        return np.asarray(w).reshape(-1, P, w.shape[1]).transpose(1, 0, 2)

    def pack(name):
        if name[:2] in ("kc", "vc", "ks", "kw", "vs", "vw"):
            return rows(col[name])
        if name[0] == "q":
            j = int(name[1])
            w = np.asarray(col["q"]).reshape(D, GROUPS, HPG, HD)[:, :, j, :].reshape(D, P)
            return rows(w)
        if name[:2] == "w1":
            w = (cmp_k_w1 if name[2] == "k" else cmp_v_w1)[0]
            return rows(w)[:, 4 * int(name[3]):4 * int(name[3]) + 4, :]
        c = int(name[1])
        return rows(col[name[0]][:, c * P:(c + 1) * P])

    def columns(a):
        return np.asarray(a).reshape(-1, P).T

    arrays = {
        "x": x,
        "ln1": columns(ln1[0]),
        "wpack": np.stack([pack(n).reshape(P, D) for n in STREAM1]),
        "pos": np.stack([np.asarray(p[0]).reshape(LPAIRS, P).T for p in (cmp_pos_k, cmp_pos_v)], axis=1),
        "wg": rows(np.asarray(col["g"]).reshape(D, HEADS, 3).transpose(0, 2, 1).reshape(D, 24)),
        "w2k": rows(np.concatenate([cmp_k_w2[0], cmp_k_w2[0]], axis=1)),
        "w2v": rows(cmp_v_w2[0]),
        "convw": np.asarray(conv_w[0]).reshape(3, CC, P).transpose(2, 1, 0),
        "gnc": columns(gn_conv[0]),
        "gna": columns(gn_attn[0]),
        "subk": np.asarray(peer_subkeys[0]).reshape(HC, P, P).transpose(2, 0, 1),
        "ln2": np.asarray(ln2),
        "lnf": np.asarray(ln_f)[None, :],
        "w_out": rows(w_out[0]),
        "wq": np.asarray(peer_wq[0]).reshape(DC, P, HC, P).transpose(2, 1, 0, 3).reshape(HC, P, D),
        "uv": np.concatenate([peer_u[0], peer_v[0]], axis=1),
    }
    arrays = {name: np.ascontiguousarray(a) for name, a in arrays.items()}
    nc = bacc.Bacc("TRN2", target_bir_lowering=False, num_devices=1)
    aps = {name: nc.dram_tensor(name + "_dram", a.shape, mybir.dt.from_np(a.dtype), kind="ExternalInput").ap()
           for name, a in arrays.items()}
    out = nc.dram_tensor("out_dram", (1, SEQ, D), F32, kind="ExternalOutput").ap()
    layer(nc, aps, out)
    r = run_bass_kernel_spmd(nc, [{name + "_dram": a for name, a in arrays.items()}], core_ids=[0])
    return r.results[0]["out_dram"]
```

```python
from contextlib import ExitStack

import numpy as np

import concourse.bass as bass
from concourse import mybir

F32 = mybir.dt.float32
F32R = mybir.dt.float32r
U32 = mybir.dt.uint32
ALU = mybir.AluOpType
ACT = mybir.ActivationFunctionType
AX_X = mybir.AxisListType.X

P = 128
SEQ, D = 512, 1024
TILES = SEQ // P
DC = D // P
HEADS, GROUPS, HD = 8, 2, 64
HPG = HEADS // GROUPS
NB = 32
NCMP = (SEQ - 32) // 16 + 1
NBLK = GROUPS * NCMP
GATES = 3 * HEADS
LPAIRS = 16
CC = 4
PH = 8
HC = 2 * PH
TOPK = 16
KTOT = PH * TOPK
EPS = 1e-6
NEG = -1e30
GELU_C = float(np.sqrt(2.0 / np.pi))
RING = 8
GRP = 4
GPE = 3
ITERS = KTOT // RING
SLOTS = 4
WQ_SLOTS = 7
KEYS = 5

STREAM1 = (["kc", "vc", "ks", "kw", "q0", "q1", "q2", "q3", "v0", "v1"]
           + ["h0", "c0", "b0"] + [f"w1k{i}" for i in range(4)] + [f"w1v{i}" for i in range(4)]
           + [f"{s}{c}" for c in range(1, CC) for s in "hcb"])
N1 = len(STREAM1)
W1_PIECES = sum(name[:2] == "w1" for name in STREAM1)
NSP = 3
SPLIT = [n for n, name in enumerate(STREAM1) if name[:2] != "w1"]

BRANCH_HEADS = [(b, h) for b in range(2) for h in (0, 4, 1, 5, 2, 6, 3, 7)]
NBH = len(BRANCH_HEADS)
CONV0 = SPLIT.index(STREAM1.index("h0"))

GAPS = 2 * ITERS - 1
START = 20


def head_at(t, i):
    return i if t % 2 == 0 else PH - 1 - i


def half_at(t, i):
    return i if t % 2 == 0 else 1 - i


def wq_plan():
    holds = {slot: None for slot in range(WQ_SLOTS)}
    filled = {slot: sum(n % SLOTS == slot for n in range(N1)) if slot < SLOTS else 0 for slot in range(WQ_SLOTS)}
    oldest = list(range(SLOTS, WQ_SLOTS)) + [n % SLOTS for n in range(N1 - SLOTS, N1)]
    replaces = {n % SLOTS: ("phase1", n) for n in range(N1 - SLOTS, N1)}
    plan = {}
    for t in range(TILES):
        for p in range(HC):
            what = 2 * head_at(t, p // 2) + half_at(t, p % 2)
            slot = next((k for k in holds if holds[k] == what), None)
            load = None
            if slot is None:
                slot = oldest[0]
                load = replaces.get(slot, ("nothing", 0))
                holds[slot] = what
                filled[slot] += 1
            oldest.remove(slot)
            oldest.append(slot)
            replaces[slot] = ("use", t * HC + p)
            plan[t, p] = (what, slot, filled[slot], load)
    return plan


def first_topk(n):
    h = n // 3
    return (19 + n // 2 if h == 0 else START + (n - 3) // 2 if h == 1 else
            START + 3 + (n - 6) * 15 // 17)


def later_topk(n):
    half = 3 * PH // 2
    return GAPS - half + n if n < half else GAPS + (n - half) * 3 // 2


def front_plan(cmp=0, topk=later_topk):
    plan = [{"pe": [], "act": [], "dve": []} for _ in range(2 * GAPS)]

    def put(gap, engine, *step):
        plan[gap][engine].append(step)

    put(cmp, "pe", "cmp_scores")
    put(cmp + 1, "dve", "cmp_shift")
    put(cmp + 1, "act", "cmp_exp")
    put(cmp + 1, "pe", "cmp_turn")
    put(cmp + 2, "dve", "cmp_coef")
    put(cmp + 2, "act", "cmp_turned")
    put(cmp + 2, "pe", "cmp_values")
    put(cmp + 3, "dve", "cmp_out")
    pairs = NBH // 2
    for gap in range(3, 3 + pairs + 2):
        two = lambda pair: (2 * pair, 2 * pair + 1) if 0 <= pair < pairs else ()
        for n in two(gap - 4):
            put(gap, "dve", "max", n)
        for n in two(gap - 5):
            put(gap, "act", "turned", n)
            put(gap, "pe", "values", n)
        for n in two(gap - 4):
            put(gap, "act", "exp", n)
            put(gap, "pe", "turn", n)
        for n in two(gap - 3):
            put(gap, "pe", "scores", n)
    put(5 + pairs // 2, "dve", "branch", 0)
    put(12, "pe", "yc", 0)
    put(12, "pe", "yc", 1)
    put(13, "dve", "branch", 1)
    put(13, "dve", "att_norm")
    put(13, "pe", "att_turn")
    put(13, "dve", "add_yc", 0)
    put(14, "dve", "att_turned")
    put(14, "dve", "add_yc", 1)
    put(14, "pe", "ya", 0)
    put(14, "pe", "ya", 1)
    put(15, "dve", "norm2")
    put(15, "pe", "x2_turn")
    put(16, "act", "x2_turned")
    put(16, "dve", "x2_scale")
    step = 1 if topk is first_topk else 2
    for h in range(PH):
        put(17 + step * h, "act", "pq_out", h)
        put(17 + step * h, "pe", "ps", h)
        put(18 + step * h, "act", "ps_out", h)
    for h in range(PH):
        put(16 + step * h, "pe", "pq", h)
    for n in range(3 * PH):
        gap, h = topk(n), n // 3
        put(gap, "dve", ("keys", "cand", "place")[n % 3], h)
        if n % 3 == 1:
            put(gap, "act", "best_exp", h)
        if n % 3 == 2:
            put(gap, "dve", "gates", h)
    return plan


def conv_plan(plan):
    for k in range(4, 3 * CC):
        plan[k - 1]["act"].insert(0, ("split", CONV0 + k))
        plan[k - 1]["dve"].append(("split", CONV0 + k))
    for c in range(1, CC):
        for k in range(3):
            plan[3 * c + k]["pe"].insert(0, ("conv", 3 * c + k))
        plan[3 * c + 1]["act"].append(("conv_in", c))
        plan[3 * c + 2]["dve"].append(("conv_mix", c))
        plan[3 * c + 3]["dve"].append(("conv_gate", c))
        plan[3 * c + 3]["act"].append(("conv_out", c))
    last = 3 * CC
    plan[last]["pe"].insert(plan[last]["pe"].index(("yc", 1)), ("conv_squares",))
    plan[last + 1]["dve"].insert(plan[last + 1]["dve"].index(("add_yc", 0)), ("conv_rstd",))


def schedule():
    plan, first = front_plan(), front_plan(4, first_topk)
    conv_plan(first)
    engines = ("pe", "act", "dve")
    done = [("place", 0), ("gates", 0)]
    ahead = [{e: [(0, s) for s in gap[e]] for e in engines} for gap in first[:START]]
    ahead.append({"pe": [], "act": [], "dve": [(0, s) for s in done]})
    inside = [[{e: [] for e in engines} for _ in range(GAPS)] for _ in range(TILES)]
    for t in range(TILES):
        for gap in range(GAPS):
            for e in engines:
                own = first[START + gap] if t == 0 else plan[GAPS + gap]
                inside[t][gap][e] += [(t, s) for s in own[e] if t or s not in done]
                if t < TILES - 1:
                    inside[t][gap][e] += [(t + 1, s) for s in plan[gap][e]]
    for t in range(1, TILES):
        inside[t][1]["dve"].append((t - 1, ("final_norm",)))
    return ahead, inside


AHEAD, INSIDE = schedule()


def wide_order():
    names = ["kc", "vc", "ks", "kw", "q0", "q1", "q2", "q3", "va", "vb", "gt", "hidk", "hidv", "kcc", "vcc"]
    for gap in AHEAD + [gap for tile in INSIDE for gap in tile]:
        for t, step in gap["pe"]:
            if step[0] == "cmp_scores":
                names += [("sc", t, 0), ("sc", t, 1)]
            elif step[0] == "cmp_values":
                names += [("oc", t)]
            elif step[0] in ("scores", "yc", "ya", "pq", "ps"):
                names += [(step[0], t, step[1])]
    return {name: n for n, name in enumerate(names)}


def turn_order():
    names = ["gt", "hid"]
    for gap in AHEAD + [gap for tile in INSIDE for gap in tile]:
        for t, step in gap["pe"]:
            if step[0] == "cmp_turn":
                names += [("pc", t)]
            elif step[0] == "turn":
                names += [("p", t, step[1])]
            elif step[0] == "att_turn":
                names += [("at", t)]
            elif step[0] == "x2_turn":
                names += [("x2", t, 0), ("x2", t, 1)]
    return {name: n for n, name in enumerate(names)}


def layer(nc, A, out):
    WIDE, TURN, wq = wide_order(), turn_order(), wq_plan()
    with ExitStack() as ctx:
        where = {}

        def sb(name, shape, dt=F32):
            where[name] = -(-nc.sbuf_base // 32) * 32
            return ctx.enter_context(nc.sbuf_tensor(name, shape, dt))

        def over(name, shape, host, at=0):
            return nc.alloc_sbuf_tensor_at(name, shape, F32R, offset=where[host] + 4 * at)

        def sem(name):
            return ctx.enter_context(nc.semaphore(name))

        wide = ctx.enter_context(nc.psum_tensor("wide", [P, 2, 512], F32))
        turn = ctx.enter_context(nc.psum_tensor("turn", [P, 2, 512], F32))
        att_ps = ctx.enter_context(nc.psum_tensor("att_ps", [P, 2, 512], F32))
        acc = ctx.enter_context(nc.psum_tensor("acc", [P, 2, 512], F32))

        x_banks = [z[:, i, :] for z in (turn, att_ps, acc, wide) for i in range(2)]

        ring = sb("ring", [P, RING, 2 * D])
        w_out = sb("w_out_sb", [P, DC, D])
        xh = sb("xh", [P, 2, D])
        xn2 = sb("xn2", [P, 2, D])
        keys_s = sb("keys_s", [P, KEYS, 2, P])
        stream = sb("stream", [P, WQ_SLOTS, D])
        subk = sb("subk", [P, HC, P])
        qT = sb("qT", [P, HPG, SEQ])
        kT = sb("kT", [P, 2, SEQ])
        vtok = sb("vtok", [P, TILES, 2, P])
        convT = sb("convT", [P, CC, SEQ])
        ln2 = sb("ln2_sb", [P, D])
        lnf = sb("lnf", [P, D])
        ident = sb("ident", [P, P])
        causal = sb("causal", [P, P])
        cmask = sb("cmask", [P, TILES, NB])
        has_c = sb("has_c", [P, 1])
        iota16 = sb("iota16", [P, TOPK])
        iota16i = sb("iota16i", [P, TOPK], mybir.dt.int32)
        mean_col = sb("mean_col", [P, 1])
        convw = sb("convw", [P, CC, 3])
        gnc = sb("gnc", [P, CC])
        gna = sb("gna", [P, CC])
        pos = sb("pos", [P, 2, LPAIRS])
        sig = sb("sig", [P, TILES, 3, HEADS])
        kcc = sb("kcc", [P, NB])
        vbd = sb("vbd", [P, GROUPS, HPG, HD])
        stat = sb("stat", [P, 8])
        newton = sb("newton", [P, 3, TILES])
        rstd_c = sb("rstd_c", [P, TILES])
        rstd_2 = sb("rstd_2", [P, 2])
        mean_x = sb("mean_x", [P, TILES])
        rstd_x = sb("rstd_x", [P, TILES])
        probs = sb("probs", [P, 2, 512])
        probsT = sb("probsT", [P, 2, 512])
        attn = sb("attn", [P, 512])
        atmp = sb("atmp", [P, 512])
        sigT = atmp[0:GATES, :]
        xT2 = probs[:, :, :].rearrange("p a b -> p (a b)")
        attT = probsT[:, 0, :]
        pq = probsT
        pcs = attn[:, 0:256].rearrange("p (g j n) -> p g j n", g=GROUPS, j=HPG)
        pcT = attn[:, 256:512].rearrange("p (g q) -> p g q", g=GROUPS)
        cmax = sb("cmax", [P, HEADS])
        csum = sb("csum", [P, HEADS])
        nmax = sb("nmax", [P, NBH])
        sums = sb("sums", [P, 2, HEADS])
        coef = sb("coef", [P, HEADS])
        cand = sb("cand", [P, TOPK, TOPK])
        onehot = atmp[:, :].rearrange("p (c k j) -> p c k j", c=2, k=TOPK)
        sv = sb("sv", [P, 2, TOPK])
        si = sb("si", [P, 2, TOPK], U32)
        sif = sb("sif", [P, 2, TOPK])
        best = sb("best", [P, TOPK])
        bi = sb("bi", [P, TOPK], U32)
        bhl = sb("bhl", [P, 2, TOPK], U32)
        bhlf = sb("bhlf", [P, 2, TOPK])
        ij = sb("ij", [P, 2, TOPK])
        bdiff = sb("bdiff", [P, TOPK])
        bexp = sb("bexp", [P, 2, TOPK])
        bsum = sb("bsum", [P, 2])
        brec = sb("brec", [P, 1])
        idx = sb("idx", [P, 2, KTOT], U32)
        gate = sb("gate", [P, 2 * KTOT])
        ph = sb("ph", [P, 2, GRP])
        pt1 = sb("pt1", [P, GRP])
        pt2 = sb("pt2", [P, GRP])
        pt3 = sb("pt3", [P, GRP])
        pth = sb("pth", [P, 2, GRP])
        pa = sb("pa", [P, 2, GRP])
        diag = sb("diag", [P, GPE, P])

        flat = ring[:, :, :].rearrange("p a b -> p (a b)")
        xs = flat[:, 0:4096].rearrange("p (t d) -> p t d", t=TILES)
        xw = ([flat[:, 4096 + t * D:4096 + (t + 1) * D] for t in range(3)]
              + [probsT[:, :, :].rearrange("p a b -> p (a b)")])
        sq_x = probs[:, :, :].rearrange("p a b -> p (a b)")
        xn = [over("xn_hi", [P, DC, SEQ], "ring", 8192), over("xn_lo", [P, DC, SEQ], "w_out_sb", CC * D)]
        w_parts = [[over(f"w_{part}{k}", [P, D], host, (at + i) * D) for i, part in enumerate(("hi", "lo"))]
                   for k, (host, at) in enumerate((("stream", SLOTS), ("xh", 0), ("xn2", 0)))]
        wg = flat[:, 7808:8000]
        wg_parts = [over("wg_hi", [P, DC, GATES], "ring", 8000), over("wg_lo", [P, DC, GATES], "ring", 4128)]
        ln1 = convT[:, 0:2, :].rearrange("p a s -> p (a s)")
        kvc = flat[:, 12288:13312].rearrange("p (a s) -> p a s", a=2)
        kv2 = flat[:, 13312:15360].rearrange("p (a g s) -> p a g s", a=2, g=GROUPS)
        kvb = flat[:, 5120:7104].rearrange("p (a m n) -> p a m n", a=2, m=LPAIRS)
        w2k = flat[:, 7424:7680].rearrange("p (h n) -> p h n", h=2)
        w2v = flat[:, 7680:7808].rearrange("p (h n) -> p h n", h=2)
        hx = flat[:, 3088:3600].rearrange("p (a h) -> p a h", a=2)
        ht = flat[:, 3600:4112].rearrange("p (a h) -> p a h", a=2)
        hidk = flat[:, 15616:15744].rearrange("p (h g n) -> p h g n", h=2, g=GROUPS)
        hidv = flat[:, 15744:16256].rearrange("p (h g j n) -> p h g j n", h=2, g=GROUPS, j=HPG)
        zc = flat[:, 0:1040].rearrange("p (a s) -> p a s", a=2)
        chs = flat[:, 1040:2064].rearrange("p (a s) -> p a s", a=2)
        cacc = flat[:, 2064:3088].rearrange("p (a s) -> p a s", a=2)
        sqc = flat[:, 3088:4112].rearrange("p (a s) -> p a s", a=2)
        sqsum = flat[:, 4112:4624]
        cout = flat[:, 6144:7168].rearrange("p (a s) -> p a s", a=2)

        params = sem("params")
        ln1_in = sem("ln1_in")
        x_in = [sem(f"x_in{t}") for t in range(TILES)]
        xh_in = [sem(f"xh_in{i}") for i in range(2)]
        w_out_in = [sem(f"w_out_in{i}") for i in range(2)]
        streamed = [sem(f"streamed{i}") for i in range(WQ_SLOTS)]
        stream_used = sem("stream_used")
        consts = sem("consts")
        wide_full = [sem(f"wide_full{i}") for i in range(2)]
        wide_free = [sem(f"wide_free{i}") for i in range(2)]
        turn_full = [sem(f"turn_full{i}") for i in range(2)]
        turn_free = [sem(f"turn_free{i}") for i in range(2)]
        vorder = sem("vorder")
        x_squared = sem("x_squared")
        rstd_ready = sem("rstd_ready")
        xw_ready = sem("xw_ready")
        xs_ready = [sem(f"xs_ready{i}") for i in range(2)]
        x_turned = sem("x_turned")
        xn_hi = sem("xn_hi")
        xn_lo = sem("xn_lo")
        w_hi = sem("w_hi")
        w_lo = sem("w_lo")
        w_parts_used = sem("w_parts_used")
        wg_hi = sem("wg_hi")
        wg_lo = sem("wg_lo")
        kvb_ready = sem("kvb_ready")
        kv2_in = sem("kv2_in")
        hid_poly = sem("hid_poly")
        hid_tanh = sem("hid_tanh")
        hid_out = sem("hid_out")
        conv_ready = sem("conv_ready")
        sq_added = sem("sq_added")
        conv_full = [sem(f"conv_full{i}") for i in range(2)]
        conv_free = [sem(f"conv_free{i}") for i in range(2)]
        cmp_shifted = sem("cmp_shifted")
        cmp_exp = sem("cmp_exp")
        max_ready = sem("max_ready")
        pv_done = sem("pv_done")
        att_free = sem("att_free")
        attn_ready = sem("attn_ready")
        keys_used = sem("keys_used")
        bdiff_ready = sem("bdiff_ready")
        bexp_ready = sem("bexp_ready")
        idx_ready = sem("idx_ready")
        xn2_ready = sem("xn2_ready")
        x2_scaled = sem("x2_scaled")
        landed = [sem(f"landed{i}") for i in range(RING)]
        h_ready = sem("h_ready")
        gelu_step = sem("gelu_step")
        tanh_ready = sem("tanh_ready")
        diag_ready = sem("diag_ready")
        combined = sem("combined")
        vcombined = sem("vcombined")
        acc_read = sem("acc_read")
        out_ready = sem("out_ready")
        out_done = sem("out_done")

        N_PARAMS = 10

        def wait_full(eng, full, use):
            eng.wait_ge(full[use % 2], use // 2 + 1)

        def wait_read(eng, free, use):
            eng.wait_ge(free[use % 2], use // 2 + 1)

        def wait_free(eng, free, use):
            if use >= 2:
                eng.wait_ge(free[use % 2], use // 2)

        block = ctx.enter_context(nc.Block())

        @block.sync
        def _(sp):
            for t in range(TILES):
                sp.dma_start(xs[:, t, :], A["x"][0, t * P:(t + 1) * P, :]).then_inc(x_in[t], 16)
                if t == 0:
                    sp.dma_start(ln1, A["ln1"].to_broadcast([P, D])).then_inc(ln1_in, 16)

            def piece(n, src):
                before = n - SLOTS
                if before in SPLIT:
                    sp.wait_ge(w_lo, SPLIT.index(before) + 1)
                elif before >= 0:
                    sp.wait_ge(stream_used, before + 1 - sum(m < before for m in SPLIT))
                sp.dma_start(stream[:, n % SLOTS, :], src).then_inc(streamed[n % SLOTS], 16)

            for n in range(SLOTS):
                piece(n, A["wpack"][n])
            for dst, name in ((pos[:], "pos"), (wg, "wg"), (w2k, "w2k"), (w2v, "w2v"), (convw[:], "convw"),
                              (gnc[:], "gnc"), (gna[:], "gna"), (subk[:], "subk")):
                sp.dma_start(dst, A[name]).then_inc(params, 16)
            sp.dma_start(ln2[:], A["ln2"].to_broadcast([P, D])).then_inc(params, 16)
            sp.dma_start(lnf[:], A["lnf"].to_broadcast([P, D])).then_inc(params, 16)
            for n in range(SLOTS, 9):
                piece(n, A["wpack"][n])
            wait_read(sp, wide_free, WIDE["kc"])
            wait_read(sp, wide_free, WIDE["vc"])
            for a in range(2):
                for g in range(GROUPS):
                    sp.dma_start(kv2[0:HD, a, g, :], kvc[g * HD:(g + 1) * HD, a, :]).then_inc(kv2_in, 16)
                    sp.dma_start(kv2[HD:P, a, g, 0:SEQ - 1], kvc[g * HD:(g + 1) * HD, a, 1:SEQ]).then_inc(kv2_in, 16)
            for n in range(9, N1):
                piece(n, A["wpack"][n])
                if n == N1 - CC:
                    sp.dma_start(w_out[:, 0:CC, :], A["w_out"][:, 0:CC, :]).then_inc(w_out_in[0], 16)

            def store(t):
                sp.wait_ge(out_ready, t + 1)
                sp.dma_start(out[0, t * P:(t + 1) * P, :], xn2[:, t % 2, :]).then_inc(out_done, 16)

            for t in range(TILES):
                if t >= 2:
                    store(t - 2)
                if t == 0:
                    wait_full(sp, conv_full, 3 * CC - 1)
                sp.dma_start(xh[:, t % 2, :], A["x"][0, t * P:(t + 1) * P, :]).then_inc(xh_in[t % 2], 16)
                if t == 0:
                    sp.dma_start(w_out[:, CC:DC, :], A["w_out"][:, CC:DC, :]).then_inc(w_out_in[1], 16)
                for p in range(HC):
                    what, slot, _, load = wq[t, p]
                    if load is None:
                        continue
                    if load[0] == "use":
                        sp.wait_ge(stream_used, W1_PIECES + load[1] + 1)
                    elif load[0] == "phase1":
                        sp.wait_ge(w_lo, SPLIT.index(load[1]) + 1)
                    sp.dma_start(stream[:, slot, :], A["wq"][what]).then_inc(streamed[slot], 16)
            for t in range(TILES - 2, TILES):
                store(t)
            sp.wait_ge(out_done, 16 * TILES)

        @block.gpsimd
        def _(pool):
            for z in (ident[:], causal[:], cmask[:], hidk, hidv, vbd[:]):
                nc.gpsimd.memset(z, 0.0).then_inc(consts, 1)
            nc.gpsimd.memset(has_c[:], 1.0).then_inc(consts, 1)
            nc.gpsimd.memset(mean_col[:], 1.0 / 512).then_inc(consts, 1)
            nc.gpsimd.iota(iota16i[:], pattern=[[1, TOPK]], base=0, channel_multiplier=0).then_inc(consts, 1)
            pool.wait_ge(consts, 9)
            nc.gpsimd.affine_select(out=ident[:], in_=ident[:], compare_op=ALU.not_equal, fill=1.0, base=0,
                                    pattern=[[-1, P]], channel_multiplier=1).then_inc(consts, 1)
            nc.gpsimd.affine_select(out=causal[:], in_=causal[:], compare_op=ALU.is_ge, fill=NEG, base=0,
                                    pattern=[[-1, P]], channel_multiplier=1).then_inc(consts, 1)
            nc.gpsimd.affine_select(out=cmask[:], in_=cmask[:], compare_op=ALU.is_ge, fill=NEG, base=-31,
                                    pattern=[[P, TILES], [-16, NB]], channel_multiplier=1).then_inc(consts, 1)
            nc.gpsimd.affine_select(out=has_c[:], in_=has_c[:], compare_op=ALU.is_ge, fill=0.0, base=-31,
                                    pattern=[[0, 1]], channel_multiplier=1).then_inc(consts, 1)
            nc.gpsimd.tensor_copy(iota16[:], iota16i[:]).then_inc(consts, 1)
            for c in range(CC):
                pool.wait_ge(conv_ready, 2 * c + 1)
                if c == 0:
                    nc.gpsimd.tensor_copy(sqsum, sqc[:, 0, :]).then_inc(sq_added, 1)
                else:
                    pool.wait_ge(sq_added, c)
                    nc.gpsimd.tensor_tensor(sqsum, sqsum, sqc[:, c % 2, :], ALU.add).then_inc(sq_added, 1)
            for t in range(TILES):
                for k in range(KTOT):
                    n = t * KTOT + k
                    if k % TOPK == 0:
                        pool.wait_ge(idx_ready, t * PH + k // TOPK + 1)
                    if n >= RING:
                        group, j = n // GRP - 2, n % GRP
                        if j < GPE:
                            pool.wait_ge(combined, GPE * group + j + 1)
                        else:
                            pool.wait_ge(vcombined, group + 1)
                    nc.gpsimd.indirect_dma_start(
                        out=ring[:, n % RING, :], out_offset=None, in_=A["uv"],
                        in_offset=bass.IndirectOffsetOnAxis(ap=idx[:, t % 2, k:k + 1], axis=0),
                    ).then_inc(landed[n % RING], 16)

        CONSTS = 14

        @block.scalar
        def _(act):
            def evac(name, dst, scale=1.0, cols=512):
                use = WIDE[name]
                wait_full(act, wide_full, use)
                nc.scalar.activation(dst, wide[:, use % 2, 0:cols], ACT.Copy, scale=scale).then_inc(wide_free[use % 2], 1)

            for t in range(TILES):
                act.wait_ge(x_in[t], 16)
                if t:
                    act.wait_ge(x_squared, t)
                nc.scalar.activation(sq_x, xs[:, t, :], ACT.Square, scale=D ** -0.5,
                                     accum_out=mean_x[:, t:t + 1]).then_inc(x_squared, 1)

            def split_hi(m):
                n = SPLIT[m]
                act.wait_ge(streamed[n % SLOTS], 16 * (n // SLOTS + 1))
                if m >= NSP:
                    act.wait_ge(w_parts_used, m - NSP + 1)
                nc.scalar.activation(w_parts[m % NSP][0][:], stream[:, n % SLOTS, :], ACT.Copy).then_inc(w_hi, 1)

            split_hi(0)
            act.wait_ge(rstd_ready, 1)
            for t in (1, 3):
                nc.scalar.activation(xw[t], xw[t], ACT.Copy, scale=rstd_x[:, t:t + 1]).then_inc(xs_ready[1], 1)
            for t in range(TILES):
                for i in range(2):
                    act.wait_ge(x_turned, 2 * t + i + 1)
                    nc.scalar.activation(xn[0][:, 4 * i:4 * i + 4, t * P:(t + 1) * P],
                                         x_banks[2 * t + i].rearrange("p (c q) -> p c q", c=4),
                                         ACT.Copy).then_inc(xn_hi, 1)
            split_hi(1)
            split_hi(2)
            act.wait_ge(params, 16 * N_PARAMS)
            nc.scalar.activation(wg_parts[0][:], wg.rearrange("p (c n) -> p c n", c=DC), ACT.Copy).then_inc(wg_hi, 1)
            act.wait_ge(consts, CONSTS)
            for a, name in enumerate(("kc", "vc")):
                evac(name, kvc[:, a, :])
                split_hi(3 + a)
            for a, name in enumerate(("ks", "kw")):
                evac(name, kT[:, a, :])
                split_hi(5 + a)
            for j in range(HPG):
                evac(f"q{j}", qT[:, j, :], scale=HD ** -0.5)
                split_hi(7 + j)
            for k, name in enumerate(("va", "vb")):
                evac(name, vtok[:, 2 * k:2 * k + 2, :, :].rearrange("p t b c -> p (t b c)"))
                split_hi(11 + k)
            use = WIDE["gt"]
            wait_full(act, wide_full, use)
            nc.scalar.activation(sigT, wide[0:GATES, use % 2, :], ACT.Exp, scale=-1.0).then_inc(wide_free[use % 2], 1)

            def hidden_tanh(a):
                act.wait_ge(hid_poly, a + 1)
                nc.scalar.activation(ht[0:NBLK, a, :], ht[0:NBLK, a, :], ACT.Tanh, scale=GELU_C).then_inc(hid_tanh, 1)

            def conv_in(c):
                if c >= 2:
                    wait_read(act, conv_free, 3 * (c - 2) + 1)
                use = 3 * c
                wait_full(act, conv_full, use)
                nc.scalar.activation(chs[:, c % 2, :], acc[:, use % 2, :], ACT.Copy).then_inc(conv_free[use % 2], 1)

            def conv_out(c):
                wait_read(act, conv_free, 3 * c + 2)
                if c >= 2:
                    act.wait_ge(sq_added, c - 1)
                nc.scalar.activation(sqc[:, c % 2, :], cout[:, c % 2, :], ACT.Square).then_inc(conv_ready, 1)
                nc.scalar.activation(convT[:, c, :], cout[:, c % 2, :], ACT.Copy,
                                     scale=gnc[:, c:c + 1]).then_inc(conv_ready, 1)

            act.wait_ge(params, 16 * N_PARAMS)
            hidden_tanh(0)
            hidden_tanh(1)
            conv_in(0)
            split_hi(CONV0 + NSP)
            use = WIDE["kcc"]
            wait_full(act, wide_full, use)
            nc.scalar.activation(kcc[0:HD, :], wide[0:HD, use % 2, 0:NB], ACT.Copy)
            nc.scalar.activation(kcc[HD:P, :], wide[HD:P, use % 2, NB:2 * NB], ACT.Copy).then_inc(wide_free[use % 2], 1)
            use = WIDE["vcc"]
            wait_full(act, wide_full, use)
            for j in range(HPG):
                rows = slice(j * NB, (j + 1) * NB)
                ins = nc.scalar.activation(vbd[rows, :, j, :],
                                           wide[rows, use % 2, 0:P].rearrange("p (g d) -> p g d", g=2), ACT.Copy)
            ins.then_inc(wide_free[use % 2], 1)
            conv_out(0)

            def probs_exp(t, n):
                keys = (t + 1) * P
                b, h = BRANCH_HEADS[n]
                use = WIDE[("scores", t, n)]
                act.wait_ge(max_ready, t * NBH + n + 1)
                if n >= 2:
                    wait_full(act, turn_full, TURN[("p", t, n - 2)])
                elif t >= 1:
                    wait_full(act, wide_full, WIDE[("pq", t - 1, PH - 1)])
                nc.scalar.activation(probs[:, n % 2, 0:keys], wide[:, use % 2, 0:keys], ACT.Exp,
                                     bias=nmax[:, n:n + 1], accum_out=sums[:, b, h:h + 1]).then_inc(wide_free[use % 2], 1)

            def probs_turn(t, n):
                keys = (t + 1) * P
                use = TURN[("p", t, n)]
                wait_full(act, turn_full, use)
                if n >= 2:
                    act.wait_ge(pv_done, t * NBH + n - 1)
                nc.scalar.activation(probsT[:, n % 2, 0:keys], turn[:, use % 2, 0:keys],
                                     ACT.Copy).then_inc(turn_free[use % 2], 1)

            def step(t, name, i=0):
                if name == "cmp_exp":
                    act.wait_ge(cmp_shifted, t + 1)
                    nc.scalar.activation(pcs, pcs, ACT.Exp).then_inc(cmp_exp, 1)
                elif name == "cmp_turned":
                    use = TURN[("pc", t)]
                    wait_full(act, turn_full, use)
                    nc.scalar.activation(pcT[:, :, :].rearrange("p g q -> p (g q)"), turn[:, use % 2, 0:2 * P],
                                         ACT.Copy).then_inc(turn_free[use % 2], 1)
                elif name == "split":
                    split_hi(i)
                elif name == "conv_in":
                    conv_in(i)
                elif name == "conv_out":
                    conv_out(i)
                elif name == "exp":
                    probs_exp(t, i)
                elif name == "turned":
                    probs_turn(t, i)
                elif name == "x2_turned":
                    for k in range(2):
                        use = TURN[("x2", t, k)]
                        wait_full(act, turn_full, use)
                        nc.scalar.activation(xT2[:, k * 512:(k + 1) * 512], turn[:, use % 2, :],
                                             ACT.Copy).then_inc(turn_free[use % 2], 1)
                elif name == "pq_out":
                    evac(("pq", t, i), pq[:, i % 2, 0:2 * P], cols=2 * P)
                elif name == "ps_out":
                    if i >= KEYS or t >= 1:
                        act.wait_ge(keys_used, PH * t + max(0, i - KEYS + 1))
                    if i == 0:
                        act.wait_ge(x2_scaled, t + 1)
                    evac(("ps", t, i), keys_s[:, i % KEYS, :, :].rearrange("p c n -> p (c n)"),
                         scale=rstd_2[:, t % 2:t % 2 + 1], cols=2 * P)
                elif name == "best_exp":
                    act.wait_ge(bdiff_ready, t * PH + i + 1)
                    nc.scalar.activation(bexp[:, i % 2, :], bdiff[:], ACT.Exp,
                                         accum_out=bsum[:, i % 2:i % 2 + 1]).then_inc(bexp_ready, 1)

            def group(i, q, first=False):
                act.wait_ge(gelu_step, 10 * i + 5 * q + 3)
                nc.scalar.activation(pth[:, q, :], pt3[:], ACT.Tanh, scale=GELU_C).then_inc(tanh_ready, 1)
                act.wait_ge(gelu_step, 10 * i + 5 * q + 5)
                for j in range(GPE):
                    if not first:
                        act.wait_ge(combined, 2 * GPE * i + GPE * q + j + 1 - GPE)
                    nc.scalar.activation(diag[:, j, :], ident[:], ACT.Copy,
                                         scale=pa[:, q, j:j + 1]).then_inc(diag_ready, 1)

            def last_group():
                i, q = TILES * ITERS - 1, 1
                for part, (lo, hi) in enumerate(((0, GPE), (GPE, GRP))):
                    act.wait_ge(gelu_step, 10 * i + 5 * q + 5 * part + 3)
                    nc.scalar.activation(pth[:, q, lo:hi], pt3[:, lo:hi], ACT.Tanh, scale=GELU_C).then_inc(tanh_ready, 1)
                    if part == 0:
                        act.wait_ge(gelu_step, 10 * i + 5 * q + 5)
                        for j in range(GPE):
                            act.wait_ge(combined, 2 * GPE * i + GPE * q + j + 1 - GPE)
                            nc.scalar.activation(diag[:, j, :], ident[:], ACT.Copy,
                                                 scale=pa[:, q, j:j + 1]).then_inc(diag_ready, 1)

            run_plan("act", step, group, nc.scalar.Fori, last_group=last_group)

        @block.tensor
        def _(pe):
            held = [None, 1]
            parts = ((0, 0), (0, 1), (1, 0))

            def piece(n):
                pe.wait_ge(streamed[n % SLOTS], 16 * (n // SLOTS + 1))
                return stream[:, n % SLOTS, :]

            def let_go(ins):
                if held[0]:
                    ins.then_inc(held[0], held[1])
                held[:] = None, 1

            def split_piece(name, chunks=DC):
                m = SPLIT.index(STREAM1.index(name))
                pe.wait_ge(w_lo, m + 1)
                return [z[:].rearrange("p (c n) -> p c n", c=chunks) for z in w_parts[m % NSP]]

            def transposes(name, srcs, rows=P):
                use = TURN[name]
                wait_free(pe, turn_free, use)
                for i, s in enumerate(srcs):
                    ins = nc.tensor.transpose(turn[:, use % 2, i * rows:(i + 1) * rows], s, ident[0:rows, 0:rows])
                ins.then_inc(turn_full[use % 2], 1)

            pe.wait_ge(consts, CONSTS)
            for t in range(TILES):
                pe.wait_ge(xs_ready[t % 2], t // 2 + 1)
                for i in range(2):
                    for c in range(4):
                        ins = nc.tensor.transpose(x_banks[2 * t + i][:, c * P:(c + 1) * P],
                                                  xw[t][:, (4 * i + c) * P:(4 * i + c + 1) * P], ident[:])
                    ins.then_inc(x_turned, 1)
            pe.wait_ge(xn_lo, 2 * TILES)

            def channels(name, banks, full, free, use):
                w = split_piece(name)
                wait_free(pe, free, use)
                for c in range(DC):
                    for a, b in parts:
                        ins = nc.tensor.matmul(banks[:, use % 2, :], w[a][:, c, :], xn[b][:, c, :],
                                               start=(c == 0 and (a, b) == parts[0]),
                                               stop=(c == DC - 1 and (a, b) == parts[-1]))
                        let_go(ins)
                ins.then_inc(full[use % 2], 1)
                held[0] = w_parts_used

            def tokens(out, t, w):
                for c in range(DC):
                    for a, b in parts:
                        ins = nc.tensor.matmul(out, xn[b][:, c, t * P:(t + 1) * P], w[c][a],
                                               start=(c == 0 and (a, b) == parts[0]),
                                               stop=(c == DC - 1 and (a, b) == parts[-1]))
                        let_go(ins)
                return ins

            for name in ("kc", "vc", "ks", "kw", "q0", "q1", "q2", "q3"):
                channels(name, wide, wide_full, wide_free, WIDE[name])
            halves = [split_piece(name, CC) for name in ("v0", "v1")]
            w = [[z[:, c % CC, :] for z in halves[c // CC]] for c in range(DC)]
            for name, first in (("va", 0), ("vb", 2)):
                use = WIDE[name]
                wait_free(pe, wide_free, use)
                for k in range(2):
                    ins = tokens(wide[:, use % 2, k * 256:(k + 1) * 256], first + k, w)
                ins.then_inc(wide_full[use % 2], 1)
            held[0], held[1] = w_parts_used, 2
            pe.wait_ge(wg_lo, 1)
            use = WIDE["gt"]
            wait_free(pe, wide_free, use)
            for c in range(DC):
                for a, b in parts:
                    ins = nc.tensor.matmul(wide[0:GATES, use % 2, :], wg_parts[a][:, c, :], xn[b][:, c, :],
                                           start=(c == 0 and (a, b) == parts[0]),
                                           stop=(c == DC - 1 and (a, b) == parts[-1]))
                    let_go(ins)
            ins.then_inc(wide_full[use % 2], 1)

            def hidden(a):
                name = "kv"[a]
                use = WIDE[f"hid{name}"]
                wait_free(pe, wide_free, use)
                pe.wait_ge(kvb_ready, a + 1)
                for m in range(LPAIRS):
                    if m % 4 == 0:
                        w = piece(STREAM1.index(f"w1{name}{m // 4}")).rearrange("p (m n) -> p m n", m=4)
                    ins = nc.tensor.matmul(wide[0:NBLK, use % 2, 0:256], kvb[:, a, m, :], w[:, m % 4, :],
                                           start=(m == 0), stop=(m == LPAIRS - 1))
                    let_go(ins)
                    held[0] = stream_used if m % 4 == 3 else None
                ins.then_inc(wide_full[use % 2], 1)

            hidden(0)
            wait_read(pe, wide_free, WIDE["gt"])
            transposes("gt", [sigT[:, t * P:(t + 1) * P] for t in range(TILES)], GATES)
            hidden(1)

            def conv(k):
                channels(f"{'hcb'[k % 3]}{k // 3}", acc, conv_full, conv_free, k)

            for k in range(2):
                conv(k)
            pe.wait_ge(hid_out, 2)
            use = TURN["hid"]
            wait_free(pe, turn_free, use)
            for a in range(2):
                for hh in range(2):
                    o = (2 * a + hh) * NBLK
                    ins = nc.tensor.transpose(turn[:, use % 2, o:o + NBLK], hx[0:NBLK, a, hh * P:(hh + 1) * P],
                                              ident[0:NBLK, 0:NBLK])
            ins.then_inc(turn_full[use % 2], 1)
            conv(2)
            wait_read(pe, turn_free, use)
            use = WIDE["kcc"]
            wait_free(pe, wide_free, use)
            for hh in range(2):
                ins = nc.tensor.matmul(wide[:, use % 2, 0:2 * NB], w2k[:, hh, :],
                                       hidk[:, hh, :, :].rearrange("p g n -> p (g n)"), start=(hh == 0), stop=(hh == 1))
            ins.then_inc(wide_full[use % 2], 1)
            use = WIDE["vcc"]
            wait_free(pe, wide_free, use)
            for g in range(GROUPS):
                for hh in range(2):
                    ins = nc.tensor.matmul(wide[:, use % 2, g * HD:(g + 1) * HD],
                                           hidv[:, hh, g, :, :].rearrange("p j n -> p (j n)"), w2v[:, hh, :],
                                           start=(hh == 0), stop=(hh == 1))
            ins.then_inc(wide_full[use % 2], 1)

            def scores(t, n):
                b, h = BRANCH_HEADS[n]
                g, j = h // HPG, h % HPG
                rows = slice(g * HD, (g + 1) * HD)
                use = WIDE[("scores", t, n)]
                wait_free(pe, wide_free, use)
                nc.tensor.matmul(wide[:, use % 2, 0:(t + 1) * P], qT[rows, j, t * P:(t + 1) * P],
                                 kT[rows, b, 0:(t + 1) * P], start=True, stop=True).then_inc(wide_full[use % 2], 1)

            def values(t, n):
                b, h = BRANCH_HEADS[n]
                use = TURN[("p", t, n)]
                wait_read(pe, turn_free, use)
                if n % HEADS == 0:
                    if t >= 1:
                        pe.wait_ge(att_free, 2 * (t - 1) + b + 1)
                for kb in range(t + 1):
                    ins = nc.tensor.matmul(att_ps[:, b, h * HD:(h + 1) * HD], probsT[:, n % 2, kb * P:(kb + 1) * P],
                                           vtok[:, kb, b, (h // HPG) * HD:(h // HPG + 1) * HD],
                                           start=(kb == 0), stop=(kb == t))
                ins.then_inc(pv_done, 1)

            def step(t, name, i=0):
                if name == "cmp_scores":
                    if t == 0:
                        wait_read(pe, wide_free, WIDE["kcc"])
                    for g in range(GROUPS):
                        use = WIDE[("sc", t, g)]
                        wait_free(pe, wide_free, use)
                        rows = slice(g * HD, (g + 1) * HD)
                        for j in range(HPG):
                            ins = nc.tensor.matmul(wide[:, use % 2, j * NB:(j + 1) * NB], qT[rows, j, t * P:(t + 1) * P],
                                                   kcc[rows, :], start=True, stop=True)
                        ins.then_inc(wide_full[use % 2], 1)
                elif name == "cmp_turn":
                    pe.wait_ge(cmp_exp, t + 1)
                    transposes(("pc", t), [pcs[:, g, :, :].rearrange("p j n -> p (j n)") for g in range(GROUPS)])
                elif name == "cmp_values":
                    wait_read(pe, turn_free, TURN[("pc", t)])
                    if t == 0:
                        wait_read(pe, wide_free, WIDE["vcc"])
                    use = WIDE[("oc", t)]
                    wait_free(pe, wide_free, use)
                    for g in range(GROUPS):
                        ins = nc.tensor.matmul(wide[:, use % 2, g * 256:(g + 1) * 256], pcT[:, g, :],
                                               vbd[:, g, :, :].rearrange("p j d -> p (j d)"), start=True, stop=True)
                    ins.then_inc(wide_full[use % 2], 1)
                elif name == "conv":
                    conv(i)
                elif name == "conv_squares":
                    pe.wait_ge(sq_added, CC)
                    use = 3 * CC
                    wait_free(pe, conv_free, use)
                    for tile in range(TILES):
                        ins = nc.tensor.matmul(acc[:, use % 2, tile:tile + 1], sqsum[:, tile * P:(tile + 1) * P],
                                               mean_col[:], start=True, stop=True)
                        let_go(ins)
                    ins.then_inc(conv_full[use % 2], 1)
                elif name == "scores":
                    scores(t, i)
                elif name == "turn":
                    wait_read(pe, wide_free, WIDE[("scores", t, i)])
                    transposes(("p", t, i), [probs[:, i % 2, kb * P:(kb + 1) * P] for kb in range(t + 1)])
                elif name == "values":
                    values(t, i)
                elif name == "att_turn":
                    pe.wait_ge(attn_ready, t + 1)
                    transposes(("at", t), [attn[:, c * P:(c + 1) * P] for c in range(CC)])
                elif name in ("yc", "ya"):
                    use = WIDE[(name, t, i)]
                    wait_free(pe, wide_free, use)
                    if t == 0:
                        pe.wait_ge(w_out_in[name == "ya"], 16)
                        pe.wait_ge(conv_ready, 2 * CC)
                    if name == "ya":
                        wait_read(pe, turn_free, TURN[("at", t)])
                    for c in range(CC):
                        lhs = convT[:, c, t * P:(t + 1) * P] if name == "yc" else attT[:, c * P:(c + 1) * P]
                        ins = nc.tensor.matmul(wide[:, use % 2, :], lhs,
                                               w_out[:, c + CC * (name == "ya"), i * 512:(i + 1) * 512],
                                               start=(c == 0), stop=(c == CC - 1))
                    ins.then_inc(wide_full[use % 2], 1)
                elif name == "x2_turn":
                    for k in range(2):
                        pe.wait_ge(xn2_ready, 2 * t + k + 1)
                        transposes(("x2", t, k), [xn2[:, t % 2, (4 * k + c) * P:(4 * k + c + 1) * P] for c in range(4)])
                elif name == "pq":
                    use = WIDE[("pq", t, i)]
                    wait_free(pe, wide_free, use)
                    for k in range(2):
                        if i == 0:
                            wait_read(pe, turn_free, TURN[("x2", t, k)])
                        for p in range(2):
                            a = half_at(t, p)
                            _, slot, filled, _ = wq[t, 2 * i + p]
                            pe.wait_ge(streamed[slot], 16 * filled)
                            w = stream[:, slot, :].rearrange("p (c n) -> p c n", c=DC)
                            for c in range(4 * k, 4 * k + 4):
                                ins = nc.tensor.matmul(wide[:, use % 2, a * P:(a + 1) * P], w[:, c, :],
                                                       xT2[:, c * P:(c + 1) * P], start=(c == 0 and p == 0),
                                                       stop=(c == DC - 1), skip_group_check=True)
                                let_go(ins)
                            held[0] = stream_used if k else None
                    ins.then_inc(wide_full[use % 2], 1)
                elif name == "ps":
                    wait_read(pe, wide_free, WIDE[("pq", t, i)])
                    use = WIDE[("ps", t, i)]
                    wait_free(pe, wide_free, use)
                    for a in range(2):
                        ins = nc.tensor.matmul(wide[:, use % 2, a * P:(a + 1) * P], pq[:, i % 2, a * P:(a + 1) * P],
                                               subk[:, 2 * head_at(t, i) + a, :], start=True, stop=True)
                        let_go(ins)
                    ins.then_inc(wide_full[use % 2], 1)

            def group(i, q, first=False, start=False, stop=False):
                for j in range(GPE):
                    pe.wait_ge(diag_ready, 2 * GPE * i + GPE * q + j + 1)
                    for half in range(2):
                        ins = nc.tensor.matmul(acc[:, half, :], diag[:, j, :],
                                               ring[:, q * GRP + j, D + half * 512:D + (half + 1) * 512],
                                               start=start and j == 0, stop=stop and j == GPE - 1,
                                               skip_group_check=True)
                    ins.then_inc(combined, 1)

            def edge(i, q):
                start, stop = (i % ITERS, q) == (0, 0), (i % ITERS, q) == (ITERS - 1, 1)
                if start and i:
                    pe.wait_ge(acc_read, 2 * (i // ITERS))
                group(i, q, start=start, stop=stop)

            run_plan("pe", step, group, nc.tensor.Fori, edge)

        @block.vector
        def _(dve):
            v = nc.vector
            count = [0]

            def then(ins):
                dve.wait_ge(vorder, mark(ins))

            def mark(ins):
                count[0] += 1
                ins.then_inc(vorder, 1)
                return count[0]

            def bcast(ap, n):
                return ap.unsqueeze(2).to_broadcast([ap.shape[0], ap.shape[1], n])

            def rstd(dst, mean, last=None):
                n = dst.shape[1]
                xh, y, e = (newton[:, k, 0:n] for k in range(3))
                then(v.tensor_scalar(xh, mean, EPS, 0.5, ALU.add, ALU.mult))
                then(v.tensor_scalar(y.bitcast(U32), xh.bitcast(U32), -0.5, float(0x5F3759DF - 0x400000 + 0x80000000),
                                     ALU.mult, ALU.add))
                for step in range(3):
                    if n == 1:
                        then(v.tensor_scalar(e, y, y, xh, ALU.mult, ALU.mult))
                    else:
                        then(v.tensor_tensor(e, y, y, ALU.mult))
                        then(v.tensor_tensor(e, e, xh, ALU.mult))
                    ins = v.scalar_tensor_tensor(dst if step == 2 else y, e, -1.5, y, ALU.add, ALU.mult)
                    if step == 2 and last is not None:
                        ins.then_inc(last, 1)
                    else:
                        then(ins)

            dve.wait_ge(consts, CONSTS)
            dve.wait_ge(ln1_in, 16)
            for t in range(TILES):
                dve.wait_ge(x_in[t], 16)
                v.tensor_tensor(xw[t], xs[:, t, :], ln1, ALU.mult).then_inc(xw_ready, 1)
            dve.wait_ge(xw_ready, TILES)
            dve.wait_ge(x_squared, TILES)
            rstd(rstd_x[:], mean_x[:], rstd_ready)
            dve.wait_ge(rstd_ready, 1)
            for t in (0, 2):
                v.tensor_scalar(xw[t], xw[t], rstd_x[:, t:t + 1], None, ALU.mult).then_inc(xs_ready[0], 1)

            def split_lo(m):
                n = SPLIT[m]
                dve.wait_ge(w_hi, m + 1)
                v.tensor_tensor(w_parts[m % NSP][1][:], stream[:, n % SLOTS, :], w_parts[m % NSP][0][:],
                                ALU.subtract).then_inc(w_lo, 1)

            split_lo(0)
            for t in range(TILES):
                for i in range(2):
                    dve.wait_ge(xn_hi, 2 * t + i + 1)
                    v.tensor_tensor(xn[1][:, 4 * i:4 * i + 4, t * P:(t + 1) * P],
                                    x_banks[2 * t + i].rearrange("p (c q) -> p c q", c=4),
                                    xn[0][:, 4 * i:4 * i + 4, t * P:(t + 1) * P],
                                    ALU.subtract).then_inc(xn_lo, 1)
            split_lo(1)
            split_lo(2)
            dve.wait_ge(wg_hi, 1)
            v.tensor_tensor(wg_parts[1][:], wg.rearrange("p (c n) -> p c n", c=DC), wg_parts[0][:],
                            ALU.subtract).then_inc(wg_lo, 1)
            then(v.memset(zc[:, :, 0:2], 0.0))

            for m in range(NSP, 8):
                split_lo(m)
            dve.wait_ge(params, 16 * N_PARAMS)
            dve.wait_ge(kv2_in, 16 * 8)
            for a in range(2):
                for g in range(GROUPS):
                    src = kv2[:, a, g, 0:SEQ]
                    for half in range(2):
                        n0 = half * 16
                        pairs = src[:, n0:n0 + 16 * NCMP].rearrange("p (n m r) -> p m n r", n=NCMP, m=8)[:, :, :, 0]
                        ins = v.tensor_tensor(kvb[:, a, 8 * half:8 * half + 8, g * NCMP:(g + 1) * NCMP], pairs,
                                              bcast(pos[:, a, 8 * half:8 * half + 8], NCMP), ALU.add)
                ins.then_inc(kvb_ready, 1)
            for m in range(8, CONV0 + NSP):
                split_lo(m)
            use = TURN["gt"]
            wait_full(dve, turn_full, use)
            sg = sig[:, :, :, :].rearrange("p t a h -> p (t a h)")
            v.tensor_scalar(sg, turn[:, use % 2, 0:TILES * GATES], 1.0, None, ALU.add).then_inc(turn_free[use % 2], 1)
            wait_read(dve, turn_free, use)
            then(v.reciprocal(sg, sg))

            def hidden(a):
                use = WIDE["hid" + "kv"[a]]
                wait_full(dve, wide_full, use)
                hxa, hta = (z[0:NBLK, a, :] for z in (hx, ht))
                v.tensor_copy(hxa, wide[0:NBLK, use % 2, 0:256]).then_inc(wide_free[use % 2], 1)
                wait_read(dve, wide_free, use)
                then(v.tensor_tensor(hta, hxa, hxa, ALU.mult))
                then(v.tensor_scalar(hta, hta, 0.044715, 1.0, ALU.mult, ALU.add))
                v.tensor_tensor(hta, hta, hxa, ALU.mult).then_inc(hid_poly, 1)

            hidden(0)
            hidden(1)
            for a in range(2):
                hxa, hta = (z[0:NBLK, a, :] for z in (hx, ht))
                dve.wait_ge(hid_tanh, a + 1)
                v.scalar_tensor_tensor(hxa, hta, 1.0, hxa, ALU.add, ALU.mult).then_inc(hid_out, 1)
            use = TURN["hid"]
            wait_full(dve, turn_full, use)
            for a in range(2):
                for hh in range(2):
                    o = (2 * a + hh) * NBLK
                    src = turn[:, use % 2, o:o + NBLK].rearrange("p (g n) -> p g n", g=GROUPS)
                    for dst in ([hidk[:, hh, :, 0:NCMP]] if a == 0 else
                                [hidv[:, hh, :, j, 0:NCMP] for j in range(HPG)]):
                        ins = v.tensor_scalar(dst, src, 0.5, None, ALU.mult)
            ins.then_inc(turn_free[use % 2], 1)

            def conv_mix(c):
                b = c % 2
                wait_read(dve, conv_free, 3 * c)
                use = 3 * c + 1
                wait_full(dve, conv_full, use)
                v.tensor_tensor(zc[:, b, 2:514], chs[:, b, :], acc[:, use % 2, :],
                                ALU.mult).then_inc(conv_free[use % 2], 1)
                wait_read(dve, conv_free, use)
                then(v.tensor_scalar(cacc[:, b, :], zc[:, b, 0:512], convw[:, c, 0:1], None, ALU.mult))
                for k in (1, 2):
                    then(v.scalar_tensor_tensor(cacc[:, b, :], zc[:, b, k:k + 512], convw[:, c, k:k + 1],
                                                cacc[:, b, :], ALU.mult, ALU.add))

            def conv_gate(c):
                use = 3 * c + 2
                wait_full(dve, conv_full, use)
                if c >= 2:
                    dve.wait_ge(conv_ready, 2 * (c - 1))
                v.tensor_tensor(cout[:, c % 2, :], cacc[:, c % 2, :], acc[:, use % 2, :],
                                ALU.mult).then_inc(conv_free[use % 2], 1)

            split_lo(CONV0 + NSP)
            conv_mix(0)
            conv_gate(0)

            def branch_out(t, b):
                dve.wait_ge(pv_done, t * NBH + HEADS * (b + 1))
                then(v.reciprocal(coef[:], sums[:, b, :]))
                then(v.tensor_tensor(coef[:], coef[:], sig[:, t, 1 + b, :], ALU.mult))
                then(v.tensor_tensor(atmp[:, :].rearrange("p (h d) -> p h d", h=HEADS),
                                     att_ps[:, b, :].rearrange("p (h d) -> p h d", h=HEADS), bcast(coef[:], HD),
                                     ALU.mult))
                v.tensor_tensor(attn[:], attn[:], atmp[:], ALU.add).then_inc(att_free, 1)
                dve.wait_ge(att_free, 2 * t + b + 1)

            def row_max(t, n):
                use = WIDE[("scores", t, n)]
                wait_full(dve, wide_full, use)
                own = wide[:, use % 2, t * P:(t + 1) * P]
                then(v.tensor_tensor(own, own, causal[:], ALU.add))
                if n == 0 and t >= 1:
                    wait_read(dve, wide_free, WIDE[("scores", t - 1, NBH - 1)])
                v.tensor_reduce(nmax[:, n:n + 1], wide[:, use % 2, 0:(t + 1) * P], AX_X, ALU.max,
                                negate=True).then_inc(max_ready, 1)

            def top16(lists):
                last = [0] * len(lists)
                for step in range(5):
                    k = 0 if step < 3 else 8
                    for n, (src, vals, inds) in enumerate(lists):
                        if step:
                            dve.wait_ge(vorder, last[n])
                        if step in (0, 3):
                            ins = v.max(vals[:, k:k + 8], src)
                        elif step == 2:
                            ins = v.match_replace(src, vals[:, 0:8], src, -3.0e38)
                        else:
                            ins = v.max_index(inds[:, k:k + 8], vals[:, k:k + 8], src)
                        last[n] = mark(ins)
                dve.wait_ge(vorder, last[-1])

            def keys(t, h):
                wait_read(dve, wide_free, WIDE[("ps", t, h)])
                top16([(keys_s[:, h % KEYS, c, :], sv[:, c, :], si[:, c, :]) for c in range(2)])

            def candidates(t, h):
                v.tensor_tensor(cand[:], bcast(sv[:, 0, :], TOPK), sv[:, 1:2, :].to_broadcast([P, TOPK, TOPK]),
                                ALU.add).then_inc(keys_used, 1)
                dve.wait_ge(keys_used, t * PH + h + 1)
                top16([(cand[:, :, :].rearrange("p a b -> p (a b)"), best[:, :], bi[:, :])])
                m = t * PH + h
                if m >= 1:
                    dve.wait_ge(bexp_ready, m)
                v.tensor_scalar(bdiff[:], best[:], best[:, 0:1], None, ALU.subtract).then_inc(bdiff_ready, 1)

            def place(t, h):
                mark(v.tensor_copy(sif[:], si[:]))
                mark(v.tensor_scalar(bhl[:, 0, :], bi[:], 4, None, ALU.logical_shift_right))
                then(v.tensor_scalar(bhl[:, 1, :], bi[:], 15, None, ALU.bitwise_and))
                then(v.tensor_copy(bhlf[:], bhl[:]))
                oh = onehot.rearrange("p c k j -> p (c k) j")
                then(v.tensor_tensor(oh, bcast(bhlf[:, :, :].rearrange("p c k -> p (c k)"), TOPK),
                                     iota16[:].unsqueeze(1).to_broadcast([P, 2 * TOPK, TOPK]), ALU.is_equal))
                then(v.tensor_tensor(onehot, onehot, sif[:].unsqueeze(2).to_broadcast([P, 2, TOPK, TOPK]),
                                     ALU.mult))
                then(v.tensor_reduce(ij[:, :, :].rearrange("p c k -> p (c k)"), oh, AX_X, ALU.add))
                v.scalar_tensor_tensor(idx[:, t % 2, h * TOPK:(h + 1) * TOPK], ij[:, 0, :], float(P), ij[:, 1, :],
                                       ALU.mult, ALU.add).then_inc(idx_ready, 1)

            def gates(t, h):
                m = t * PH + h
                dve.wait_ge(bexp_ready, m + 1)
                then(v.reciprocal(brec[:], bsum[:, h % 2:h % 2 + 1]))
                g = (m % (2 * PH)) * TOPK
                then(v.tensor_scalar(gate[:, g:g + TOPK], bexp[:, h % 2, :], brec[:], 0.5, ALU.mult,
                                     ALU.mult))

            def step(t, name, i=0):
                xhh = xh[:, t % 2, i * 512:(i + 1) * 512] if i < 2 else None
                if name == "cmp_shift":
                    for g in range(GROUPS):
                        use = WIDE[("sc", t, g)]
                        wait_full(dve, wide_full, use)
                        v.tensor_tensor(pcs[:, g, :, :], wide[:, use % 2, 0:P].rearrange("p (j n) -> p j n", j=HPG),
                                        cmask[:, t:t + 1, :].to_broadcast([P, HPG, NB]),
                                        ALU.add).then_inc(wide_free[use % 2], 1)
                        wait_read(dve, wide_free, use)
                    heads = pcs[:, :, :, :].rearrange("p g j n -> p (g j) n")
                    then(v.tensor_reduce(cmax[:], heads, AX_X, ALU.max))
                    v.tensor_tensor(heads, heads, bcast(cmax[:], NB), ALU.subtract).then_inc(cmp_shifted, 1)
                elif name == "cmp_coef":
                    dve.wait_ge(cmp_exp, t + 1)
                    then(v.tensor_reduce(csum[:], pcs[:, :, :, :].rearrange("p g j n -> p (g j) n"), AX_X, ALU.add))
                    then(v.reciprocal(coef[:], csum[:]))
                    then(v.tensor_tensor(coef[:], coef[:], sig[:, t, 0, :], ALU.mult))
                    if t == 0:
                        then(v.tensor_scalar(coef[:], coef[:], has_c[:], None, ALU.mult))
                elif name == "cmp_out":
                    use = WIDE[("oc", t)]
                    wait_full(dve, wide_full, use)
                    v.tensor_tensor(attn[:, :].rearrange("p (h d) -> p h d", h=HEADS),
                                    wide[:, use % 2, :].rearrange("p (h d) -> p h d", h=HEADS), bcast(coef[:], HD),
                                    ALU.mult).then_inc(wide_free[use % 2], 1)
                    wait_read(dve, wide_free, use)
                elif name == "split":
                    split_lo(i)
                elif name == "conv_mix":
                    conv_mix(i)
                elif name == "conv_gate":
                    conv_gate(i)
                elif name == "conv_rstd":
                    use = 3 * CC
                    wait_full(dve, conv_full, use)
                    v.tensor_copy(rstd_c[:], acc[:, use % 2, 0:TILES]).then_inc(conv_free[use % 2], 1)
                    wait_read(dve, conv_free, use)
                    rstd(rstd_c[:], rstd_c[:])
                elif name == "max":
                    row_max(t, i)
                elif name == "branch":
                    branch_out(t, i)
                elif name == "att_norm":
                    then(v.tensor_tensor_reduce(atmp[:], attn[:], attn[:], 1.0 / 512, 0.0, ALU.mult, ALU.add,
                                                stat[:, 0:1]))
                    rstd(stat[:, 1:2], stat[:, 0:1])
                    v.tensor_scalar(attn[:], attn[:], stat[:, 1:2], None, ALU.mult).then_inc(attn_ready, 1)
                elif name == "att_turned":
                    use = TURN[("at", t)]
                    wait_full(dve, turn_full, use)
                    v.tensor_tensor(attT.rearrange("p (c q) -> p c q", c=CC),
                                    turn[:, use % 2, :].rearrange("p (c q) -> p c q", c=CC), bcast(gna[:], P),
                                    ALU.mult).then_inc(turn_free[use % 2], 1)
                elif name == "add_yc":
                    if i == 0:
                        dve.wait_ge(xh_in[t % 2], 16 * (t // 2 + 1))
                    use = WIDE[("yc", t, i)]
                    wait_full(dve, wide_full, use)
                    v.scalar_tensor_tensor(xhh, wide[:, use % 2, :], rstd_c[:, t:t + 1], xhh, ALU.mult,
                                           ALU.add).then_inc(wide_free[use % 2], 1)
                elif name == "norm2":
                    if t >= 2:
                        dve.wait_ge(out_done, 16 * (t - 1))
                    for half in range(2):
                        cols = slice(half * 512, (half + 1) * 512)
                        use = WIDE[("ya", t, half)]
                        wait_full(dve, wide_full, use)
                        wait_read(dve, wide_free, WIDE[("yc", t, half)])
                        v.tensor_tensor(xh[:, t % 2, cols], xh[:, t % 2, cols], wide[:, use % 2, :],
                                        ALU.add).then_inc(wide_free[use % 2], 1)
                        wait_read(dve, wide_free, use)
                        v.tensor_tensor(xn2[:, t % 2, cols], xh[:, t % 2, cols], ln2[:, cols],
                                        ALU.mult).then_inc(xn2_ready, 1)
                    for half in range(2):
                        h1 = xh[:, t % 2, half * 512:(half + 1) * 512]
                        then(v.tensor_tensor_reduce(atmp[:], h1, h1, 1.0 / D, 0.0, ALU.mult, ALU.add,
                                                    stat[:, half:half + 1]))
                    then(v.tensor_tensor(stat[:, 0:1], stat[:, 0:1], stat[:, 1:2], ALU.add))
                    rstd(rstd_2[:, t % 2:t % 2 + 1], stat[:, 0:1])
                elif name == "x2_scale":
                    for k in range(2):
                        wait_full(dve, turn_full, TURN[("x2", t, k)])
                    v.tensor_scalar(xn2[:, t % 2, :], xn2[:, t % 2, :], rstd_2[:, t % 2:t % 2 + 1], None,
                                    ALU.mult).then_inc(x2_scaled, 1)
                    dve.wait_ge(x2_scaled, t + 1)
                elif name == "final_norm":
                    final_norm(t)
                elif name == "keys":
                    keys(t, i)
                elif name == "cand":
                    candidates(t, i)
                elif name == "place":
                    place(t, i)
                elif name == "gates":
                    gates(t, i)

            def group(i, q, first=False, t=None):
                xt = xn2[:, t % 2, :]
                for j in range(GRP):
                    s = q * GRP + j
                    dve.wait_ge(landed[s], 16 * i + 16)
                    v.tensor_tensor_reduce(ring[:, s, 0:D], ring[:, s, 0:D], xt, 1.0, 0.0, ALU.mult, ALU.add,
                                           ph[:, q, j:j + 1]).then_inc(h_ready, 1)
                dve.wait_ge(h_ready, 8 * i + 4 * q + 4)
                v.tensor_tensor(pt1[:], ph[:, q, :], ph[:, q, :], ALU.mult).then_inc(gelu_step, 1)
                dve.wait_ge(gelu_step, 10 * i + 5 * q + 1)
                v.tensor_scalar(pt2[:], pt1[:], 0.044715, 1.0, ALU.mult, ALU.add).then_inc(gelu_step, 1)
                dve.wait_ge(gelu_step, 10 * i + 5 * q + 2)
                v.tensor_tensor(pt3[:], pt2[:], ph[:, q, :], ALU.mult).then_inc(gelu_step, 1)
                dve.wait_ge(tanh_ready, 2 * i + q + 1)
                v.scalar_tensor_tensor(pt2[:], pth[:, q, :], 1.0, ph[:, q, :], ALU.add, ALU.mult).then_inc(gelu_step, 1)
                dve.wait_ge(gelu_step, 10 * i + 5 * q + 4)
                v.tensor_tensor(pa[:, q, :], pt2[:], gate[:, bass.ds((i - (t - t % 2) * ITERS) * RING + q * GRP, GRP)],
                                ALU.mult).then_inc(gelu_step, 1)
                dve.wait_ge(gelu_step, 10 * i + 5 * q + 5)
                if not first:
                    dve.wait_ge(vcombined, 2 * i + q)
                v.scalar_tensor_tensor(xh[:, t % 2, :], ring[:, q * GRP + GPE, D:2 * D], pa[:, q, GPE:GPE + 1],
                                       xh[:, t % 2, :], ALU.mult, ALU.add).then_inc(vcombined, 1)

            def last_group(t):
                i, q = TILES * ITERS - 1, 1
                for part, (lo, hi) in enumerate(((0, GPE), (GPE, GRP))):
                    for j in range(lo, hi):
                        s = q * GRP + j
                        dve.wait_ge(landed[s], 16 * i + 16)
                        v.tensor_tensor_reduce(ring[:, s, 0:D], ring[:, s, 0:D], xn2[:, t % 2, :], 1.0, 0.0, ALU.mult,
                                               ALU.add, ph[:, q, j:j + 1]).then_inc(h_ready, 1)
                    base = 10 * i + 5 * q + 5 * part
                    h, c1, c2, c3, a = ph[:, q, lo:hi], pt1[:, lo:hi], pt2[:, lo:hi], pt3[:, lo:hi], pa[:, q, lo:hi]
                    dve.wait_ge(h_ready, 8 * i + 4 * q + hi)
                    v.tensor_tensor(c1, h, h, ALU.mult).then_inc(gelu_step, 1)
                    dve.wait_ge(gelu_step, base + 1)
                    v.tensor_scalar(c2, c1, 0.044715, 1.0, ALU.mult, ALU.add).then_inc(gelu_step, 1)
                    dve.wait_ge(gelu_step, base + 2)
                    v.tensor_tensor(c3, c2, h, ALU.mult).then_inc(gelu_step, 1)
                    dve.wait_ge(tanh_ready, 2 * i + q + 1 + part)
                    v.scalar_tensor_tensor(c2, pth[:, q, lo:hi], 1.0, h, ALU.add, ALU.mult).then_inc(gelu_step, 1)
                    dve.wait_ge(gelu_step, base + 4)
                    g = ((i - (t - t % 2) * ITERS) * RING + q * GRP)
                    v.tensor_tensor(a, c2, gate[:, g + lo:g + hi], ALU.mult).then_inc(gelu_step, 1)
                    dve.wait_ge(gelu_step, base + 5)
                dve.wait_ge(vcombined, 2 * i + q)
                v.scalar_tensor_tensor(xh[:, t % 2, :], ring[:, q * GRP + GPE, D:2 * D], pa[:, q, GPE:GPE + 1],
                                       xh[:, t % 2, :], ALU.mult, ALU.add).then_inc(vcombined, 1)

            def finish(t):
                dve.wait_ge(combined, (t + 1) * 2 * ITERS * GPE)
                dve.wait_ge(vcombined, (t + 1) * 2 * ITERS)
                for half in range(2):
                    cols = slice(half * 512, (half + 1) * 512)
                    v.tensor_tensor(xh[:, t % 2, cols], xh[:, t % 2, cols], acc[:, half, :],
                                    ALU.add).then_inc(acc_read, 1)
                dve.wait_ge(acc_read, 2 * (t + 1))
                if t == TILES - 1:
                    final_norm(t)

            def final_norm(t):
                h1 = xh[:, t % 2, :]
                then(v.tensor_tensor_reduce(xn2[:, t % 2, :], h1, h1, 1.0 / D, 0.0, ALU.mult, ALU.add, stat[:, 2:3]))
                rstd(stat[:, 2:3], stat[:, 2:3])
                v.scalar_tensor_tensor(xn2[:, t % 2, :], h1, stat[:, 2:3], lnf[:], ALU.mult,
                                       ALU.mult).then_inc(out_ready, 1)

            run_plan("dve", step, group, nc.vector.Fori, finish=finish, last_group=lambda: last_group(TILES - 1))


def run_plan(engine, step, group, fori, edge=None, finish=None, last_group=None):
    def one(t, i, q):
        if last_group is not None and (i, q) == (TILES * ITERS - 1, 1):
            last_group()
            return
        if edge is not None and (i % ITERS, q) in ((0, 0), (ITERS - 1, 1)):
            edge(i, q)
        elif finish is not None:
            group(i, q, first=(i + q == 0), t=t)
        else:
            group(i, q, first=(i + q == 0))

    for gap in AHEAD:
        for tile, s in gap[engine]:
            step(tile, *s)
    for t in range(TILES):
        steps = {g: INSIDE[t][g][engine] for g in range(GAPS)}
        n = 0
        while n < 2 * ITERS:
            end = n
            while end < 2 * ITERS and not (end > n and steps.get(end - 1)) and not (
                    (edge or (last_group and t == TILES - 1)) and end == 2 * ITERS - 1):
                end += 1
            iters = (end - n) // 2
            if n % 2 == 0 and iters >= 2 and n > 0:
                with fori(t * ITERS + n // 2, t * ITERS + n // 2 + iters) as i:
                    for q in range(2):
                        group(i, q, **({"t": t} if finish is not None else {}))
                n += 2 * iters
            else:
                one(t, t * ITERS + n // 2, n % 2)
                n += 1
            for tile, s in steps.get(n - 1, []):
                step(tile, *s)
        if finish is not None:
            finish(t)


def kernel(x, ln1, w_in, conv_w, cmp_pos_k, cmp_pos_v, cmp_k_w1, cmp_k_w2, cmp_v_w1, cmp_v_w2,
           gn_conv, gn_attn, w_out, ln2, peer_wq, peer_subkeys, peer_u, peer_v, ln_f):
    import concourse.bacc as bacc
    from concourse.bass_utils import run_bass_kernel_spmd

    col = {}
    at = 0
    for name, n in (("h", 512), ("b", 512), ("c", 512), ("q", 512), ("kc", 128), ("vc", 128), ("ks", 128), ("vs", 128),
                    ("kw", 128), ("vw", 128), ("g", 24)):
        col[name] = w_in[0][:, at:at + n]
        at += n

    def rows(w):
        return np.asarray(w).reshape(-1, P, w.shape[1]).transpose(1, 0, 2)

    def pack(name):
        if name in ("kc", "vc", "ks", "kw"):
            return rows(col[name])
        if name[0] == "v":
            w = rows(np.concatenate([col["vs"], col["vw"]], axis=1))
            return w[:, CC * int(name[1]):CC * (int(name[1]) + 1), :]
        if name[0] == "q":
            j = int(name[1])
            w = np.asarray(col["q"]).reshape(D, GROUPS, HPG, HD)[:, :, j, :].reshape(D, P)
            return rows(w)
        if name[:2] == "w1":
            w = (cmp_k_w1 if name[2] == "k" else cmp_v_w1)[0]
            return rows(w)[:, 4 * int(name[3]):4 * int(name[3]) + 4, :]
        c = int(name[1])
        return rows(col[name[0]][:, c * P:(c + 1) * P])

    def columns(a):
        return np.asarray(a).reshape(-1, P).T

    arrays = {
        "x": x,
        "ln1": np.asarray(ln1),
        "wpack": np.stack([pack(n).reshape(P, D) for n in STREAM1]),
        "pos": np.stack([np.asarray(p[0]).reshape(LPAIRS, P).T for p in (cmp_pos_k, cmp_pos_v)], axis=1),
        "wg": rows(np.asarray(col["g"]).reshape(D, HEADS, 3).transpose(0, 2, 1).reshape(D, 24)),
        "w2k": rows(np.concatenate([cmp_k_w2[0], cmp_k_w2[0]], axis=1)),
        "w2v": rows(cmp_v_w2[0]),
        "convw": np.asarray(conv_w[0]).reshape(3, CC, P).transpose(2, 1, 0),
        "gnc": columns(gn_conv[0]),
        "gna": columns(gn_attn[0]),
        "subk": np.asarray(peer_subkeys[0]).reshape(HC, P, P).transpose(2, 0, 1),
        "ln2": np.asarray(ln2),
        "lnf": np.asarray(ln_f)[None, :],
        "w_out": rows(w_out[0]),
        "wq": np.asarray(peer_wq[0]).reshape(DC, P, HC, P).transpose(2, 1, 0, 3).reshape(HC, P, D),
        "uv": np.concatenate([peer_u[0], peer_v[0]], axis=1),
    }
    arrays = {name: np.ascontiguousarray(a) for name, a in arrays.items()}
    nc = bacc.Bacc("TRN2", target_bir_lowering=False, num_devices=1)
    aps = {name: nc.dram_tensor(name + "_dram", a.shape, mybir.dt.from_np(a.dtype), kind="ExternalInput").ap()
           for name, a in arrays.items()}
    out = nc.dram_tensor("out_dram", (1, SEQ, D), F32, kind="ExternalOutput").ap()
    layer(nc, aps, out)
    r = run_bass_kernel_spmd(nc, [{name + "_dram": a for name, a in arrays.items()}], core_ids=[0])
    return r.results[0]["out_dram"]
```
